# Optimizing a Trainium2 kernel written in Bass

```python
import jax, jax.numpy as jnp
from jax import lax
import numpy as np
import math

D_MODEL = 1024
BATCH = 1
SEQ = 512
DEPTH = 1

HGRN_KDIM = 128
HGRN_VDIM = 128
HGRN_HEADS = D_MODEL // HGRN_KDIM
HGRN_WIDTH = HGRN_HEADS * HGRN_KDIM
GLA_CHUNK = 64
SG_CHUNK = 128
SG_GROUP_CH = 128
SG_GROUPS = D_MODEL // SG_GROUP_CH
SG_WIDTH = SG_GROUPS * SG_GROUP_CH
IN_SPLITS = (HGRN_WIDTH, HGRN_WIDTH, HGRN_WIDTH, HGRN_WIDTH, HGRN_WIDTH,
             SG_WIDTH, SG_WIDTH, SG_WIDTH, D_MODEL, D_MODEL)
IN_WIDTH = 5 * HGRN_WIDTH + 3 * SG_WIDTH + 2 * D_MODEL
RMS_EPS = 1e-6
LN_EPS = 1e-5
LB_FLOOR = 1e-20


def _rmsnorm(x, w, eps=RMS_EPS):
    xf = x.astype(jnp.float32)
    y = xf * lax.rsqrt(jnp.mean(xf * xf, axis=-1, keepdims=True) + eps)
    return (y * w.astype(jnp.float32)).astype(x.dtype)

def _layernorm(x, w, b, eps=LN_EPS):
    xf = x.astype(jnp.float32)
    mu = jnp.mean(xf, axis=-1, keepdims=True)
    var = jnp.mean(jnp.square(xf - mu), axis=-1, keepdims=True)
    y = (xf - mu) * lax.rsqrt(var + eps)
    return (y * w.astype(jnp.float32) + b.astype(jnp.float32)).astype(x.dtype)

def _gla_chunked(q, k, v, log_f):
    b, h, s, dk = q.shape
    dv = v.shape[-1]
    n = s // GLA_CHUNK

    def to_chunks(t):
        return jnp.moveaxis(t.reshape(b, h, n, GLA_CHUNK, t.shape[-1]), 2, 0)

    qc, kc, vc = to_chunks(q), to_chunks(k), to_chunks(v)
    gc = jnp.cumsum(to_chunks(log_f), axis=-2)
    mask = jnp.tril(jnp.ones((GLA_CHUNK, GLA_CHUNK), dtype=bool))[:, :, None]

    def step(state, xs):
        qb, kb, vb, gb = xs
        diff = gb[..., :, None, :] - gb[..., None, :, :]
        decay = jnp.where(mask, jnp.exp(jnp.where(mask, diff, 0.0)), 0.0)
        attn = jnp.einsum('bhtd,bhsd,bhtsd->bhts', qb, kb, decay)
        o = jnp.einsum('bhts,bhsv->bhtv', attn, vb)
        o = o + jnp.einsum('bhtd,bhdv->bhtv', qb * jnp.exp(gb), state)
        g_last = gb[..., -1:, :]
        k_dec = kb * jnp.exp(g_last - gb)
        state = state * jnp.exp(g_last[..., 0, :])[..., None] + jnp.einsum('bhsd,bhsv->bhdv', k_dec, vb)
        return state, o

    state0 = jnp.zeros((b, h, dk, dv), jnp.float32)
    _, outs = lax.scan(step, state0, (qc, kc, vc, gc))
    return jnp.moveaxis(outs, 0, 2).reshape(b, h, s, dv)

def _hgrn2_forget(f_raw, lb):
    z = f_raw.astype(jnp.float32)
    k = (1.0 - lb) * jax.nn.sigmoid(-z)
    log_f = jnp.logaddexp(jnp.log(jnp.maximum(lb, LB_FLOOR)),
                          jnp.log1p(-lb) + jax.nn.log_sigmoid(z))
    return k, log_f

def _hgrn2_branch(q_raw, ffwd_raw, fbwd_raw, i_raw, g_raw, lb_fwd, lb_bwd, gnorm_w):
    b, s, _ = q_raw.shape

    def heads(t):
        return t.reshape(b, s, HGRN_HEADS, -1).transpose(0, 2, 1, 3).astype(jnp.float32)

    def flip(t):
        return jnp.flip(t, axis=2)

    q = heads(jax.nn.silu(q_raw)) * (HGRN_KDIM ** -0.5)
    v = heads(i_raw)
    k_f, g_f = _hgrn2_forget(ffwd_raw, lb_fwd)
    k_b, g_b = _hgrn2_forget(fbwd_raw, lb_bwd)
    o_fwd = _gla_chunked(q, heads(k_f), v, heads(g_f))
    o_bwd = flip(_gla_chunked(flip(q), flip(heads(k_b)), flip(v), flip(heads(g_b))))
    o = (o_fwd + o_bwd).transpose(0, 2, 1, 3)
    o = _rmsnorm(o, gnorm_w).reshape(b, s, HGRN_HEADS * HGRN_VDIM)
    return (o * jax.nn.silu(g_raw.astype(jnp.float32))).astype(q_raw.dtype)

def _spatial_gating_branch(u_raw, v_raw, g_raw, ln_w, ln_b, w_s, b_s):
    b, s, _ = u_raw.shape
    u = jax.nn.gelu(u_raw)
    v = _layernorm(jax.nn.gelu(v_raw), ln_w, ln_b)
    vc = v.reshape(b, s // SG_CHUNK, SG_CHUNK, SG_GROUPS, SG_GROUP_CH)
    mixed = jnp.einsum('gts,bnsgc->bntgc', w_s, vc) + b_s.T[None, None, :, :, None]
    return u * mixed.reshape(b, s, SG_WIDTH) * jax.nn.silu(g_raw)

def first_inputs(seed: int = 0) -> dict:
    key = jax.random.key(seed)
    ks = jax.random.split(key, 16)
    f32 = jnp.float32
    x = jax.random.normal(ks[0], (BATCH, SEQ, D_MODEL), f32)
    norm_w = 1.0 + 0.05 * jax.random.normal(ks[1], (DEPTH, D_MODEL), f32)
    w_in = jax.random.normal(ks[2], (DEPTH, D_MODEL, IN_WIDTH), f32) * D_MODEL ** -0.5
    lower_bounds = 0.1 * jax.random.normal(ks[3], (DEPTH, 2, HGRN_WIDTH), f32)
    gnorm_w = 1.0 + 0.05 * jax.random.normal(ks[4], (DEPTH, HGRN_VDIM), f32)
    ln_w = 1.0 + 0.05 * jax.random.normal(ks[5], (DEPTH, SG_WIDTH), f32)
    ln_b = 0.02 * jax.random.normal(ks[6], (DEPTH, SG_WIDTH), f32)
    w_s = jax.random.normal(ks[7], (DEPTH, SG_GROUPS, SG_CHUNK, SG_CHUNK), f32) * SG_CHUNK ** -0.5
    b_s = 1.0 + 0.1 * jax.random.normal(ks[8], (DEPTH, SG_GROUPS, SG_CHUNK), f32)
    w_proj_a = jax.random.normal(ks[9], (DEPTH, HGRN_WIDTH, D_MODEL), f32) * HGRN_WIDTH ** -0.5
    w_proj_b = jax.random.normal(ks[10], (DEPTH, SG_WIDTH, D_MODEL), f32) * SG_WIDTH ** -0.5
    w_out = jax.random.normal(ks[11], (DEPTH, D_MODEL, D_MODEL), f32) * D_MODEL ** -0.5
    final_norm_w = 1.0 + 0.05 * jax.random.normal(ks[12], (D_MODEL,), f32)
    return {"x": x, "norm_w": norm_w, "w_in": w_in, "lower_bounds": lower_bounds,
            "gnorm_w": gnorm_w, "ln_w": ln_w, "ln_b": ln_b, "w_s": w_s, "b_s": b_s,
            "w_proj_a": w_proj_a, "w_proj_b": w_proj_b, "w_out": w_out,
            "final_norm_w": final_norm_w}

def first_block(x, norm_w, w_in, lower_bounds, gnorm_w, ln_w, ln_b, w_s, b_s,
              w_proj_a, w_proj_b, w_out, final_norm_w):
    lb = jax.nn.softmax(lower_bounds.astype(jnp.float32), axis=0)
    lb = jnp.cumsum(lb, axis=0) - lb[0]
    split_points = []
    acc = 0
    for size in IN_SPLITS[:-1]:
        acc += size
        split_points.append(acc)
    for layer in range(DEPTH):
        h = _rmsnorm(x, norm_w[layer])
        proj = jnp.einsum('bsd,de->bse', h, w_in[layer])
        (q_raw, ffwd_raw, fbwd_raw, i_raw, ga_raw,
         u_raw, v_raw, gb_raw, ma_raw, mb_raw) = jnp.split(proj, split_points, axis=-1)
        y_a = _hgrn2_branch(q_raw, ffwd_raw, fbwd_raw, i_raw, ga_raw,
                            lb[layer, 0], lb[layer, 1], gnorm_w[layer])
        y_b = _spatial_gating_branch(u_raw, v_raw, gb_raw, ln_w[layer], ln_b[layer],
                                     w_s[layer], b_s[layer])
        merged = (jax.nn.sigmoid(ma_raw) * jnp.einsum('bsw,wd->bsd', y_a, w_proj_a[layer])
                  + jax.nn.sigmoid(mb_raw) * jnp.einsum('bsw,wd->bsd', y_b, w_proj_b[layer]))
        x = x + jnp.einsum('bsd,de->bse', merged, w_out[layer])
    return _rmsnorm(x, final_norm_w)


CHUNK = 64
MIX_WIDTH = D_MODEL
POOL_WIDTH = MIX_WIDTH // 2
POOL_WINDOWS = (2, 4, 8, 16)
POOL_GROUP = POOL_WIDTH // len(POOL_WINDOWS)
ATTN_HEADS = 8
HEAD_DIM = (MIX_WIDTH - POOL_WIDTH) // ATTN_HEADS
ATTN_WIDTH = ATTN_HEADS * HEAD_DIM
IDX_HEADS = 8
IDX_DIM = 64
TOPK_MAX = 256
Q_BLOCK = 128
ROPE_THETA = 10000.0
MEM_TOKENS = 256
MEM_HEADS = 4
MEM_HEAD_DIM = 128
MEM_WIDTH = MEM_HEADS * MEM_HEAD_DIM
N_GROUPS = 4
EXPERTS_PER_GROUP = 8
EXPERT_FF = 256
TOP_K_EXPERTS = 2
EPS = 1e-6
OFF_POOL = 0
OFF_Q = OFF_POOL + POOL_WIDTH
OFF_K = OFF_Q + ATTN_WIDTH
OFF_V = OFF_K + ATTN_WIDTH
OFF_QI = OFF_V + ATTN_WIDTH
OFF_KI = OFF_QI + IDX_HEADS * IDX_DIM
OFF_WI = OFF_KI + IDX_DIM
IN_COLS = OFF_WI + IDX_HEADS


def rmsnorm(x, g):
    xf = x.astype(jnp.float32)
    y = xf * lax.rsqrt(jnp.mean(xf * xf, axis=-1, keepdims=True) + EPS)
    return (y * g.astype(jnp.float32)).astype(x.dtype)

def rope_tables(seq_len, dim):
    inv = ROPE_THETA ** (-jnp.arange(0, dim, 2, dtype=jnp.float32) / dim)
    ang = jnp.arange(seq_len, dtype=jnp.float32)[:, None] * inv[None, :]
    ang = jnp.concatenate([ang, ang], axis=-1)
    return jnp.cos(ang), jnp.sin(ang)

def apply_rope(x, cos, sin):
    xf = x.astype(jnp.float32)
    half = xf.shape[-1] // 2
    rot = jnp.concatenate([-xf[..., half:], xf[..., :half]], axis=-1)
    return (xf * cos[None, :, None, :] + rot * sin[None, :, None, :]).astype(x.dtype)

def pool_mixer(u, pool_w, pool_scale):
    B, S, _ = u.shape
    uf = u.astype(jnp.float32)
    pos1 = jnp.arange(1, S + 1)
    outs = []
    for g, w in enumerate(POOL_WINDOWS):
        ug = uf[..., g * POOL_GROUP:(g + 1) * POOL_GROUP]
        cs = jnp.cumsum(ug, axis=1)
        lag = jnp.pad(cs, ((0, 0), (w, 0), (0, 0)))[:, :S]
        cnt = jnp.minimum(pos1, w).astype(jnp.float32)[None, :, None]
        mixed = ((cs - lag) / cnt - ug).astype(u.dtype)
        outs.append(jnp.einsum('bsc,cd->bsd', mixed, pool_w[g]))
    return jnp.concatenate(outs, axis=-1) * pool_scale

def dsa_attention(q, k, v, qi, ki, wi):
    B, S, H, Dh = q.shape
    topk = min(TOPK_MAX, S // 4)
    n_blocks = S // Q_BLOCK
    key_chunk = jnp.arange(S) // CHUNK
    idx_scale = (IDX_DIM ** -0.5) * (IDX_HEADS ** -0.5)
    gather = jax.vmap(lambda a, ix: a[ix])

    def block(i):
        start = i * Q_BLOCK
        qb = lax.dynamic_slice_in_dim(q, start, Q_BLOCK, axis=1)
        qib = lax.dynamic_slice_in_dim(qi, start, Q_BLOCK, axis=1)
        wib = lax.dynamic_slice_in_dim(wi, start, Q_BLOCK, axis=1)
        q_chunk = (start + jnp.arange(Q_BLOCK)) // CHUNK
        adm = key_chunk[None, :] <= q_chunk[:, None]
        rel = jax.nn.relu(jnp.einsum('bthd,bsd->bths', qib, ki).astype(jnp.float32))
        score = jnp.einsum('bths,bth->bts', rel, wib.astype(jnp.float32)) * idx_scale
        score = jnp.where(adm[None], score, -jnp.inf)
        _, sel = lax.top_k(score, topk)
        valid = key_chunk[sel] <= q_chunk[None, :, None]
        ks = gather(k, sel)
        vs = gather(v, sel)
        s = jnp.einsum('bthd,btkhd->bthk', qb, ks).astype(jnp.float32) * (Dh ** -0.5)
        s = jnp.where(valid[:, :, None, :], s, -jnp.inf)
        p = jax.nn.softmax(s, axis=-1).astype(v.dtype)
        return jnp.einsum('bthk,btkhd->bthd', p, vs)

    out = lax.map(block, jnp.arange(n_blocks))
    return out.transpose(1, 0, 2, 3, 4).reshape(B, S, H * Dh)

def memory_cross_attention(h, mem, g_mem, w_q, w_kv, q_norm, k_norm, w_o):
    B, S, _ = h.shape
    M = mem.shape[1]
    m = rmsnorm(mem, g_mem)
    q = (h @ w_q).reshape(B, S, MEM_HEADS, MEM_HEAD_DIM)
    kv = (m @ w_kv).reshape(B, M, 2, MEM_HEADS, MEM_HEAD_DIM)
    q = rmsnorm(q, q_norm)
    k = rmsnorm(kv[:, :, 0], k_norm)
    v = kv[:, :, 1]
    s = jnp.einsum('bshd,bmhd->bhsm', q, k).astype(jnp.float32) * (MEM_HEAD_DIM ** -0.5)
    p = jax.nn.softmax(s, axis=-1).astype(v.dtype)
    o = jnp.einsum('bhsm,bmhd->bshd', p, v).reshape(B, S, MEM_WIDTH)
    return o @ w_o

def hierarchical_moe(h, wg_router, bg_router, we_router, be_router, w_gate, w_up, w_down):
    B, S, D = h.shape
    hf = h.reshape(B * S, D)
    g_logits = (hf @ wg_router + bg_router).astype(jnp.float32)
    g_prob = jax.nn.softmax(g_logits, axis=-1)
    g_sel = jnp.argmax(g_logits, axis=-1)
    g_w = jnp.take_along_axis(g_prob, g_sel[:, None], axis=1)
    e_logits = (hf @ we_router + be_router).astype(jnp.float32)
    e_logits = e_logits.reshape(-1, N_GROUPS, EXPERTS_PER_GROUP)
    e_in = jnp.take_along_axis(e_logits, g_sel[:, None, None], axis=1)[:, 0]
    top_v, top_i = lax.top_k(e_in, TOP_K_EXPERTS)
    top_w = jax.nn.softmax(top_v, axis=-1) * g_w
    exp_w = jnp.sum(jax.nn.one_hot(top_i, EXPERTS_PER_GROUP, dtype=jnp.float32)
                    * top_w[..., None], axis=1)
    gates = jax.nn.one_hot(g_sel, N_GROUPS, dtype=jnp.float32)[:, :, None] * exp_w[:, None, :]
    out = jnp.zeros_like(hf)
    for g in range(N_GROUPS):
        a = jnp.einsum('nd,edf->nef', hf, w_gate[g])
        b = jnp.einsum('nd,edf->nef', hf, w_up[g])
        hid = jax.nn.silu(a) * b * gates[:, g, :, None].astype(hf.dtype)
        out = out + jnp.einsum('nef,efd->nd', hid, w_down[g])
    return out.reshape(B, S, D)

def second_inputs(seed: int = 0) -> dict:
    key = jax.random.key(seed)
    ks = jax.random.split(key, 32)
    f32 = jnp.float32
    L = DEPTH

    def nrm(k, shape, scale):
        return jax.random.normal(k, shape, f32) * scale

    def gain(k, shape):
        return 1.0 + 0.02 * jax.random.normal(k, shape, f32)

    return {
        "x": nrm(ks[0], (BATCH, SEQ, D_MODEL), 1.0),
        "mem": nrm(ks[1], (BATCH, MEM_TOKENS, D_MODEL), 1.0),
        "mix_norm": gain(ks[2], (L, D_MODEL)),
        "w_in": nrm(ks[3], (L, D_MODEL, IN_COLS), D_MODEL ** -0.5),
        "pool_w": nrm(ks[4], (L, len(POOL_WINDOWS), POOL_GROUP, POOL_GROUP), POOL_GROUP ** -0.5),
        "pool_scale": gain(ks[5], (L, POOL_WIDTH)),
        "q_norm": gain(ks[6], (L, HEAD_DIM)),
        "k_norm": gain(ks[7], (L, HEAD_DIM)),
        "idx_k_norm": gain(ks[8], (L, IDX_DIM)),
        "w_out": nrm(ks[9], (L, MIX_WIDTH, D_MODEL), MIX_WIDTH ** -0.5),
        "xattn_norm": gain(ks[10], (L, D_MODEL)),
        "mem_norm": gain(ks[11], (L, D_MODEL)),
        "xattn_wq": nrm(ks[12], (L, D_MODEL, MEM_WIDTH), D_MODEL ** -0.5),
        "xattn_wkv": nrm(ks[13], (L, D_MODEL, 2 * MEM_WIDTH), D_MODEL ** -0.5),
        "xattn_q_norm": gain(ks[14], (L, MEM_HEAD_DIM)),
        "xattn_k_norm": gain(ks[15], (L, MEM_HEAD_DIM)),
        "xattn_wo": nrm(ks[16], (L, MEM_WIDTH, D_MODEL), MEM_WIDTH ** -0.5),
        "ffn_norm": gain(ks[17], (L, D_MODEL)),
        "router_group_w": nrm(ks[18], (L, D_MODEL, N_GROUPS), D_MODEL ** -0.5),
        "router_group_b": nrm(ks[19], (L, N_GROUPS), 0.01),
        "router_expert_w": nrm(ks[20], (L, D_MODEL, N_GROUPS * EXPERTS_PER_GROUP), D_MODEL ** -0.5),
        "router_expert_b": nrm(ks[21], (L, N_GROUPS * EXPERTS_PER_GROUP), 0.01),
        "expert_w_gate": nrm(ks[22], (L, N_GROUPS, EXPERTS_PER_GROUP, D_MODEL, EXPERT_FF), D_MODEL ** -0.5),
        "expert_w_up": nrm(ks[23], (L, N_GROUPS, EXPERTS_PER_GROUP, D_MODEL, EXPERT_FF), D_MODEL ** -0.5),
        "expert_w_down": nrm(ks[24], (L, N_GROUPS, EXPERTS_PER_GROUP, EXPERT_FF, D_MODEL), EXPERT_FF ** -0.5),
    }

def second_block(x, mem, mix_norm, w_in, pool_w, pool_scale, q_norm, k_norm, idx_k_norm, w_out,
              xattn_norm, mem_norm, xattn_wq, xattn_wkv, xattn_q_norm, xattn_k_norm, xattn_wo,
              ffn_norm, router_group_w, router_group_b, router_expert_w, router_expert_b,
              expert_w_gate, expert_w_up, expert_w_down):
    B, S, _ = x.shape
    cos_a, sin_a = rope_tables(S, HEAD_DIM)
    cos_i, sin_i = rope_tables(S, IDX_DIM)
    for l in range(DEPTH):
        h = rmsnorm(x, mix_norm[l])
        z = h @ w_in[l]
        u = z[..., OFF_POOL:OFF_Q]
        q = z[..., OFF_Q:OFF_K].reshape(B, S, ATTN_HEADS, HEAD_DIM)
        k = z[..., OFF_K:OFF_V].reshape(B, S, ATTN_HEADS, HEAD_DIM)
        v = z[..., OFF_V:OFF_QI].reshape(B, S, ATTN_HEADS, HEAD_DIM)
        qi = z[..., OFF_QI:OFF_KI].reshape(B, S, IDX_HEADS, IDX_DIM)
        ki = z[..., OFF_KI:OFF_WI]
        wi = z[..., OFF_WI:IN_COLS]
        q = apply_rope(rmsnorm(q, q_norm[l]), cos_a, sin_a)
        k = apply_rope(rmsnorm(k, k_norm[l]), cos_a, sin_a)
        qi = apply_rope(qi, cos_i, sin_i)
        ki = apply_rope(rmsnorm(ki, idx_k_norm[l])[:, :, None, :], cos_i, sin_i)[:, :, 0]
        y_pool = pool_mixer(u, pool_w[l], pool_scale[l])
        y_attn = dsa_attention(q, k, v, qi, ki, wi)
        x = x + jnp.concatenate([y_pool, y_attn], axis=-1) @ w_out[l]
        h = rmsnorm(x, xattn_norm[l])
        x = x + memory_cross_attention(h, mem, mem_norm[l], xattn_wq[l], xattn_wkv[l],
                                       xattn_q_norm[l], xattn_k_norm[l], xattn_wo[l])
        h = rmsnorm(x, ffn_norm[l])
        x = x + hierarchical_moe(h, router_group_w[l], router_group_b[l], router_expert_w[l],
                                 router_expert_b[l], expert_w_gate[l], expert_w_up[l],
                                 expert_w_down[l])
    return x


def setup_inputs(seed=0):
    out = dict(first_inputs(seed))
    for name, value in second_inputs(seed + 1).items():
        if name != "x":
            out[name + "_2"] = value
    return out


def reference(
    x, norm_w, w_in, lower_bounds, gnorm_w, ln_w, ln_b, w_s, b_s, w_proj_a, w_proj_b, w_out,
    final_norm_w, mem_2, mix_norm_2, w_in_2, pool_w_2, pool_scale_2, q_norm_2, k_norm_2,
    idx_k_norm_2, w_out_2, xattn_norm_2, mem_norm_2, xattn_wq_2, xattn_wkv_2, xattn_q_norm_2,
    xattn_k_norm_2, xattn_wo_2, ffn_norm_2, router_group_w_2, router_group_b_2,
    router_expert_w_2, router_expert_b_2, expert_w_gate_2, expert_w_up_2, expert_w_down_2,
):
    x = first_block(
        x, norm_w, w_in, lower_bounds, gnorm_w, ln_w, ln_b, w_s, b_s, w_proj_a, w_proj_b, w_out,
        final_norm_w,
    )
    return second_block(
        x, mem_2, mix_norm_2, w_in_2, pool_w_2, pool_scale_2, q_norm_2, k_norm_2, idx_k_norm_2,
        w_out_2, xattn_norm_2, mem_norm_2, xattn_wq_2, xattn_wkv_2, xattn_q_norm_2,
        xattn_k_norm_2, xattn_wo_2, ffn_norm_2, router_group_w_2, router_group_b_2,
        router_expert_w_2, router_expert_b_2, expert_w_gate_2, expert_w_up_2, expert_w_down_2,
    )


_drawn_inputs = setup_inputs


def setup_inputs(seed=0):
    import zlib

    import numpy as np

    out = dict(_drawn_inputs(seed))
    spreads = {}
    factors = {'ln_b': 3.783,
     'q_norm_2': 5.612,
     'k_norm_2': 4.76,
     'idx_k_norm_2': 3.475,
     'xattn_norm_2': 5.247,
     'mem_norm_2': 4.311,
     'xattn_q_norm_2': 5.267,
     'xattn_k_norm_2': 7.776,
     'router_group_b_2': 19.16,
     'router_expert_b_2': 35.247,
     'ffn_norm_2': 8.0}
    for name, (base, spread) in spreads.items():
        noise = np.random.default_rng([zlib.crc32(name.encode()), seed]).standard_normal(out[name].shape)
        drawn = base * np.exp(spread * noise) if base else spread * noise
        out[name] = __import__('jax').numpy.asarray(drawn.astype(out[name].dtype))
    for name, factor in factors.items():
        out[name] = (out[name] * factor).astype(out[name].dtype)
    return out
```

```python
from contextlib import ExitStack

import numpy as np
import concourse.bass as bass
from concourse import mybir

ALU = mybir.AluOpType
ACT = mybir.ActivationFunctionType
AX_X = mybir.AxisListType.X
F32 = mybir.dt.float32
I32 = mybir.dt.int32

P = 128
T = 512
D = 1024
KT = D // P
NB = T // P
HEADS = 8
RMS_EPS = 1e-6
LN_EPS = 1e-5
LB_FLOOR = 1e-20
LN_SHIFT = 32
LEVELS = 7
SLOTS = 12
SEL = 128
MEM = 256
FF = 256
EXPERTS = 32
EPG = 8
REPLACED = -3.0e38
HIDDEN = -1.0e38
MASKED = -1.0e30

COLS = {}


def _cols(name, n):
    COLS[name] = sum(COLS_N.values())
    COLS_N[name] = n


COLS_N = {}
for _name, _n in (("norm_w", 8), ("lb", 16), ("gnorm", 1), ("final", 8), ("mix", 8), ("pool_scale", 4),
                  ("q_norm", 1), ("k_norm", 1), ("idx_norm", 1), ("xattn", 8), ("mem", 8), ("xq_norm", 1),
                  ("xk_norm", 1), ("ffn", 8)):
    _cols(_name, _n)
NCOLS = sum(COLS_N.values())


class Chain:

    def __init__(self, eng, sem):
        self.eng, self.sem, self.n = eng, sem, 0

    def __call__(self, ins):
        ins.then_inc(self.sem, 1)
        self.n += 1
        self.eng.wait_ge(self.sem, self.n)

    def restart(self):
        self.eng.wait_ge(self.sem, self.n)
        self.eng.sem_clear(self.sem)
        self.n = 0


def flat(ap):
    return ap.rearrange("p a c -> p (a c)")


class Core:

    def __init__(self, nc, ctx, dram):
        self.nc, self.ctx, self.dram = nc, ctx, dram
        self.names = 0
        self.scope, self.held = ExitStack(), []
        self.W = ctx.enter_context(nc.sbuf_tensor("weight_slots", [P, SLOTS, KT * P], F32))
        self.w_in = [ctx.enter_context(nc.semaphore(f"weight_slot_{j}")) for j in range(SLOTS)]
        self.w_n = [0] * SLOTS

    def sem(self, name):
        self.names += 1
        handle = self.scope.enter_context(self.nc.semaphore(f"{name}_{self.names}"))
        self.held.append(handle)
        return handle

    def recycle(self):
        runs = []
        for n in sorted(h.num for h in self.held):
            if runs and runs[-1][1] == n:
                runs[-1][1] = n + 1
            else:
                runs.append([n, n + 1])
        with self.nc.Block() as block:
            @block.gpsimd
            def _(pool):
                for a, b in runs:
                    pool.sem_clear(range(a, b))
        self.scope.close()
        self.scope, self.held = ExitStack(), []

    def slot(self, j):
        return self.W[:, j, :].rearrange("p (k c) -> p k c", c=P)

    def wide(self, j, n, c):
        return self.W[:, j:j + n, :].rearrange("p s c -> p (s c)").rearrange("p (k c) -> p k c", c=c)


def load_constants(core, ctx):
    nc, dram = core.nc, core.dram
    core.ones = ctx.enter_context(nc.sbuf_tensor("ones", [P, P], F32))
    core.ident = ctx.enter_context(nc.sbuf_tensor("ident", [P, P], F32))
    core.cols = ctx.enter_context(nc.sbuf_tensor("cols", [P, NCOLS], F32))
    core.eps = ctx.enter_context(nc.sbuf_tensor("eps", [P, 2], F32))
    core.spare = ctx.enter_context(nc.sbuf_tensor("spare", [P, 4], F32))
    core.xT = ctx.enter_context(nc.sbuf_tensor("xT", [P, KT, T], F32))
    core.hT = ctx.enter_context(nc.sbuf_tensor("hT", [P, KT, T], F32))
    loaded = core.sem("constants_loaded")
    with nc.Block() as block:
        @block.sync
        def _(sp):
            sp.dma_start(core.xT[:], dram["xT"][:]).then_inc(loaded, 16)
            sp.dma_start(core.cols[:], dram["cols"][:]).then_inc(loaded, 16)
            sp.dma_start(core.ident[:], dram["ident"][:]).then_inc(loaded, 16)
            sp.wait_ge(loaded, 48)

        @block.vector
        def _(dve):
            nc.vector.memset(core.spare[:], 0.0)
            nc.vector.memset(core.ones[:], 1.0)
            nc.vector.memset(core.eps[:, 0:1], RMS_EPS)
            nc.vector.memset(core.eps[:, 1:2], LN_EPS)


def col(core, name, k=0):
    c = COLS[name] + k
    return core.cols[:, c:c + 1]


def rms_norm(core, src, dst, kt, n, weight):
    nc = core.nc
    sq_ready, sum_ready, rs_ready = core.sem("sq_ready"), core.sem("sum_ready"), core.sem("rs_ready")
    with (nc.sbuf_tensor(f"sq{core.names}", [P, kt, n], F32) as sq,
          nc.sbuf_tensor(f"rs{core.names}", [P, n], F32) as rs,
          nc.psum_tensor(f"sum{core.names}", [P, 512], F32) as total, nc.Block() as block):
        @block.scalar
        def _(act):
            for k in range(kt):
                nc.scalar.activation(sq[:, k], src[:, k], ACT.Square).then_inc(sq_ready, 1)
            act.wait_ge(sum_ready, 1)
            nc.scalar.activation(rs[:], total[:, 0:n], ACT.Ln, bias=core.eps[:, 0:1],
                                 scale=1.0 / (kt * P)).then_inc(rs_ready, 1)
            act.wait_ge(rs_ready, 1)
            nc.scalar.activation(rs[:], rs[:], ACT.Exp, scale=-0.5).then_inc(rs_ready, 1)

        @block.tensor
        def _(pe):
            for k in range(kt):
                pe.wait_ge(sq_ready, k + 1)
                last = nc.tensor.matmul(total[:, 0:n], core.ones[:], sq[:, k], start=(k == 0), stop=(k == kt - 1))
            last.then_inc(sum_ready, 1)

        @block.vector
        def _(dve):
            dve.wait_ge(rs_ready, 2)
            for k in range(kt):
                nc.vector.scalar_tensor_tensor(out=dst[:, k], in0=src[:, k], scalar=col(core, weight, k),
                                               in1=rs[:], op0=ALU.mult, op1=ALU.mult)


def gla_stage(core, yaT):
    nc, dram, hT = core.nc, core.dram, core.hT
    QKV = 5
    F_, B_, Q_, G_, V_ = range(QKV)
    scale = float(P) ** -0.5
    with ExitStack() as ctx:
        def sb(name, shape, dt=F32):
            return ctx.enter_context(nc.sbuf_tensor("gla_" + name, shape, dt))

        def ps(name, shape):
            return ctx.enter_context(nc.psum_tensor("gla_" + name, shape, F32))

        raw = sb("raw", [P, QKV, T])
        ls = sb("log_sigmoid", [P, 4, T])
        kk = sb("keys", [P, 2, T])
        dd = sb("log_f", [P, 2, T])
        mm_ = sb("log_max", [P, 2, T])
        CB = sb("cum", [P, 2, T])
        X = sb("edge", [P, 4, T])
        qs = sb("q", [P, T])
        sg = sb("gate", [P, T])
        Tl = sb("level_decay", [P, 2, 2, T])
        QL = sb("level_q", [P, LEVELS, T])
        KL = sb("level_k", [P, LEVELS + 1, T])
        A = sb("scores", [P, NB, P])
        vn = sb("v", [P, NB, P])
        kn = sb("k_to_edge", [P, 6, P])
        S = sb("states", [P, 6, P])
        ed = sb("edge_decay", [P, 2, NB])
        sq = sb("sq", [P, T])
        rs = sb("rs", [P, T])
        scan0 = sb("scan_keep", [P, T])
        masks = sb("level_masks", [P, LEVELS + 1, P], I32)
        ln1 = sb("log_one_minus_lb", [P, 16])
        lnf = sb("log_floor", [P, 16])
        lnd = sb("log_diff", [P, 16])
        pj = ps("proj", [P, 2, 512])
        pA = ps("level", [P, 2, 512])
        pT = ps("turned", [P, 2, 512])
        pO = ps("out", [P, 512])
        pS = ps("sum", [P, 512])

        aux = core.sem("aux_loaded")
        proj_done, evac = core.sem("proj_done"), core.sem("evacuated")
        vT_done, vn_ready = core.sem("v_turned"), core.sem("v_ready")
        ln_done, ls_ready, kexp = core.sem("ln_done"), core.sem("ls_ready"), core.sem("k_ready")
        x_ready, ex_ready, kd_ready = core.sem("edge_log"), core.sem("edge_exp"), core.sem("edge_ready")
        t_ready, e_ready, lv_ready = core.sem("level_log"), core.sem("level_exp"), core.sem("level_ready")
        lvl_done, merged = core.sem("level_done"), core.sem("level_merged")
        kT_done, kn_ready, kv_done, st_ready = (core.sem(n) for n in ("k_turned", "kn_ready", "kv_done", "state"))
        o_done, sq_done, ss_done, rs_done, y_done = (core.sem(n) for n in ("o_done", "sq", "ss", "rs", "y_done"))
        lbs, dch, ach = core.sem("lower_bounds"), core.sem("dve_chain"), core.sem("act_chain")
        w0 = list(core.w_n)

        with nc.Block() as block:
            @block.sync
            def _(sp):
                sp.dma_start(scan0[:], dram["scan_keep"][:]).then_inc(aux, 16)
                sp.dma_start(masks[:], dram["level_masks"][:]).then_inc(aux, 16)
                for j in range(QKV):
                    sp.dma_start(core.W[:, j, :], dram["w_gla"][0:1, :, j, :].rearrange("h p c -> p (h c)"))\
                        .then_inc(core.w_in[j], 16)
                with sp.Fori(0, HEADS - 1) as i:
                    nxt = sp.snap(i + 1)
                    for j in range(QKV):
                        src = dram["w_gla"][bass.ds(nxt, 1), :, j, :].rearrange("h p c -> p (h c)")
                        sp.wait_ge(proj_done, i * QKV + (j + 1))
                        sp.dma_start(core.W[:, j, :], src).then_inc(core.w_in[j], 16)

            def project(pe, j, w_value, evac_value):
                pe.wait_ge(core.w_in[j], w_value)
                if evac_value is not None:
                    pe.wait_ge(evac, evac_value)
                for k in range(KT):
                    last = nc.tensor.matmul(pj[:, j % 2, :], core.slot(j)[:, k, :], hT[:, k, :],
                                            start=(k == 0), stop=(k == KT - 1))
                last.then_inc(proj_done, 1)

            def turn_v(pe, i):
                pe.wait_ge(evac, i * QKV + QKV)
                pe.wait_ge(st_ready, i + 1)
                for c in range(NB):
                    last = nc.tensor.transpose(pT[:, 0, c * P:(c + 1) * P], raw[:, V_, c * P:(c + 1) * P],
                                               core.ident[:])
                last.then_inc(vT_done, 1)

            def attend(pe, i):
                pe.wait_ge(kd_ready, i + 1)
                pe.wait_ge(vn_ready, i + 1)
                for n in range(6):
                    d, c = n // 3, n % 3 + n // 3
                    last = nc.tensor.transpose(pT[:, n // 4, (n % 4) * P:(n % 4 + 1) * P],
                                               X[:, 1 + 2 * d, c * P:(c + 1) * P], core.ident[:])
                last.then_inc(kT_done, 1)
                for l in range(LEVELS + 1):
                    pe.wait_ge(lv_ready, i * (LEVELS + 1) + (l + 1))
                    pe.wait_ge(merged, i * (LEVELS + 1) + (l + 1))
                    for c in range(NB):
                        q = QL[:, l, c * P:(c + 1) * P] if l < LEVELS else qs[:, c * P:(c + 1) * P]
                        last = nc.tensor.matmul(pA[:, l % 2, c * P:(c + 1) * P], KL[:, l, c * P:(c + 1) * P], q,
                                                start=True, stop=True)
                    last.then_inc(lvl_done, 1)
                    if l == 2:
                        pe.wait_ge(kn_ready, i + 1)
                        for n in range(6):
                            c = n % 3 + n // 3
                            last = nc.tensor.matmul(pT[:, n // 4, (n % 4) * P:(n % 4 + 1) * P], kn[:, n, :],
                                                    vn[:, c, :], start=True, stop=True)
                        last.then_inc(kv_done, 1)
                pe.wait_ge(merged, i * (LEVELS + 1) + (LEVELS + 3))
                pe.wait_ge(st_ready, i + 2)
                pe.wait_ge(y_done, i + 1)
                for c in range(NB):
                    o = pO[:, c * P:(c + 1) * P]
                    nc.tensor.matmul(o, vn[:, c, :], A[:, c, :], start=True, stop=False)
                    if c > 0:
                        last = nc.tensor.matmul(o, S[:, c - 1, :], X[:, 0, c * P:(c + 1) * P],
                                                start=False, stop=(c == NB - 1))
                    if c < NB - 1:
                        last = nc.tensor.matmul(o, S[:, 3 + c, :], X[:, 2, c * P:(c + 1) * P],
                                                start=False, stop=True)
                last.then_inc(o_done, 1)
                pe.wait_ge(sq_done, i + 1)
                nc.tensor.matmul(pS[:], core.ones[:], sq[:], start=True, stop=True).then_inc(ss_done, 1)

            @block.tensor
            def _(pe):
                for j in range(QKV):
                    project(pe, j, w0[j] + 16, j - 1 if j >= 2 else None)
                with pe.Fori(0, HEADS - 1) as i:
                    turn_v(pe, i)
                    for j in range(QKV):
                        done = (QKV, QKV - 1, QKV + 1, QKV + 2, QKV + 3)[j]
                        project(pe, j, i * 16 + (w0[j] + 32), i * QKV + done)
                    attend(pe, i)
                turn_v(pe, HEADS - 1)
                attend(pe, HEADS - 1)

            def evacuate(act, j, value):
                act.wait_ge(proj_done, value)
                nc.scalar.copy(raw[:, j], pj[:, j % 2, :]).then_inc(evac, 1)

            def act_head(act, i, chain, h, more):
                act.wait_ge(evac, i * QKV + 4)
                chain(nc.scalar.activation(ls[:], raw[:, 0:4], ACT.Abs))
                chain(nc.scalar.activation(ls[:], ls[:], ACT.Exp, scale=-1.0))
                nc.scalar.activation(ls[:], ls[:], ACT.Ln, bias=1.0).then_inc(ln_done, 1)
                act.wait_ge(ls_ready, i + 1)
                for d in range(2):
                    nc.scalar.activation(kk[:, d], kk[:, d], ACT.Exp, bias=ln1[:, bass.ds(h[d], 1)])
                chain(nc.scalar.activation(dd[:], dd[:], ACT.Abs))
                chain(nc.scalar.activation(dd[:], dd[:], ACT.Exp, scale=-1.0))
                chain(nc.scalar.activation(dd[:], dd[:], ACT.Ln, bias=1.0))
                nc.scalar.activation(ls[:, 2:4], ls[:, 2:4], ACT.Exp).then_inc(kexp, 1)
                act.wait_ge(x_ready, i + 1)
                nc.scalar.activation(X[:], X[:], ACT.Exp).then_inc(ex_ready, 1)
                for l in range(LEVELS):
                    act.wait_ge(t_ready, i * LEVELS + (l + 1))
                    nc.scalar.activation(Tl[:, l % 2], Tl[:, l % 2], ACT.Exp).then_inc(e_ready, 1)
                    if more and l in (1, 2, 4, 5):
                        j = (1, 2, 4, 5).index(l)
                        evacuate(act, j, i * QKV + (QKV + j + 1))
                if more:
                    act.wait_ge(vT_done, i + 1)
                    evacuate(act, V_, i * QKV + 2 * QKV)
                act.wait_ge(kT_done, i + 1)
                nc.scalar.copy(kn[:, 0:4].rearrange("p n c -> p (n c)"), pT[:, 0, :])
                nc.scalar.copy(kn[:, 4:6].rearrange("p n c -> p (n c)"), pT[:, 1, 0:2 * P]).then_inc(kn_ready, 1)
                act.wait_ge(o_done, i + 1)
                nc.scalar.activation(sq[:], pO[:], ACT.Square).then_inc(sq_done, 1)
                act.wait_ge(ss_done, i + 1)
                chain(nc.scalar.activation(rs[:], pS[:], ACT.Ln, bias=core.eps[:, 0:1], scale=1.0 / P))
                nc.scalar.activation(rs[:], rs[:], ACT.Exp, scale=-0.5).then_inc(rs_done, 1)

            @block.scalar
            def _(act):
                chain = Chain(act, ach)
                act.wait_ge(lbs, 1)
                nc.scalar.activation(lnf[:], lnf[:], ACT.Exp).then_inc(lbs, 1)
                act.wait_ge(lbs, 3)
                nc.scalar.activation(ln1[:], lnd[:], ACT.Ln, bias=1.0, scale=-1.0).then_inc(lbs, 1)
                nc.scalar.activation(lnf[:], lnf[:], ACT.Ln, scale=float(2 ** LN_SHIFT)).then_inc(lbs, 1)
                act.wait_ge(lbs, 7)
                for j in range(QKV):
                    evacuate(act, j, j + 1)
                with act.Fori(0, HEADS - 1) as i:
                    h = [act.snap(i), act.snap(i + HEADS)]
                    act_head(act, i, chain, h, True)
                    chain.restart()
                act_head(act, HEADS - 1, chain, [HEADS - 1, 2 * HEADS - 1], False)

            def dve_head(dve, i, chain, h):
                dve.wait_ge(vT_done, i + 1)
                nc.vector.tensor_copy(vn[:].rearrange("p n c -> p (n c)"), pT[:, 0, :]).then_inc(vn_ready, 1)
                dve.wait_ge(ln_done, i + 1)
                chain(nc.vector.scalar_tensor_tensor(out=ls[:], in0=raw[:, 0:4], scalar=0.0, in1=ls[:],
                                                     op0=ALU.min, op1=ALU.subtract))
                for d in range(2):
                    nc.vector.tensor_scalar(mm_[:, d], ls[:, d], ln1[:, bass.ds(h[d], 1)], lnf[:, bass.ds(h[d], 1)],
                                            ALU.add, ALU.max)
                    nc.vector.tensor_scalar(dd[:, d], ls[:, d], lnd[:, bass.ds(h[d], 1)], None, ALU.add)
                nc.vector.tensor_tensor(kk[:], ls[:, 0:2], raw[:, 0:2], ALU.subtract).then_inc(ls_ready, 1)
                dve.wait_ge(kexp, i + 1)
                nc.vector.scalar_tensor_tensor(out=qs[:], in0=raw[:, Q_], scalar=scale, in1=ls[:, 2],
                                               op0=ALU.mult, op1=ALU.mult)
                nc.vector.tensor_tensor(sg[:], raw[:, G_], ls[:, 3], ALU.mult)
                chain(nc.vector.tensor_tensor(dd[:], dd[:], mm_[:], ALU.add))
                nc.vector.tensor_tensor_scan(CB[:, 0], scan0[:], dd[:, 0], 0.0, ALU.mult, ALU.add)
                chain(nc.vector.tensor_tensor_scan(CB[:, 1], scan0[:], dd[:, 1], 0.0, ALU.mult, ALU.add))
                C = CB[:, 0].rearrange("p (n t) -> p n t", t=P)
                Bi = CB[:, 1].rearrange("p (n t) -> p n t", t=P)
                Xv = X[:].rearrange("p x (n t) -> p x n t", t=P)
                last_c = C[:, :, P - 1:P].to_broadcast([P, NB, P])
                nc.vector.tensor_copy(X[:, 0], CB[:, 0])
                nc.vector.tensor_tensor(Xv[:, 1], last_c, C, ALU.subtract)
                nc.vector.tensor_tensor(X[:, 3], CB[:, 1], dd[:, 1], ALU.subtract)
                chain(nc.vector.tensor_copy(ed[:, 0], Bi[:, :, P - 1]))
                nc.vector.tensor_tensor(Xv[:, 2], ed[:, 0].unsqueeze(2).to_broadcast([P, NB, P]), Xv[:, 3],
                                        ALU.subtract)
                nc.vector.tensor_copy(CB[:, 1], X[:, 3]).then_inc(x_ready, 1)
                dve.wait_ge(x_ready, i + 1)
                nc.vector.tensor_tensor(KL[:, LEVELS], kk[:, 0], kk[:, 1], ALU.add)

                def level_log(l):
                    half = P >> (l + 1)
                    v = CB[:].rearrange("p d (n u t) -> p d n u t", u=2, t=half)
                    o = Tl[:, l % 2].rearrange("p d (n u t) -> p d n u t", u=2, t=half)
                    n = T // (2 * half)
                    fr = v[:, 0, :, 0, half - 1:half].to_broadcast([P, n, half])
                    br = v[:, 1, :, 1, 0:1].to_broadcast([P, n, half])
                    nc.vector.tensor_tensor(o[:, 0, :, 0], fr, v[:, 0, :, 0], ALU.subtract)
                    nc.vector.tensor_tensor(o[:, 0, :, 1], v[:, 0, :, 1], fr, ALU.subtract)
                    nc.vector.tensor_tensor(o[:, 1, :, 0], br, v[:, 1, :, 0], ALU.subtract)
                    nc.vector.tensor_tensor(o[:, 1, :, 1], v[:, 1, :, 1], br, ALU.subtract).then_inc(t_ready, 1)

                def level_scale(l):
                    half = P >> (l + 1)
                    dve.wait_ge(e_ready, i * LEVELS + (l + 1))

                    def side(ap, u):
                        return ap.rearrange("p (n u t) -> p n u t", u=2, t=half)[:, :, u]
                    nc.vector.tensor_tensor(side(QL[:, l], 0), side(qs[:], 0), side(Tl[:, l % 2, 1], 0), ALU.mult)
                    nc.vector.tensor_tensor(side(QL[:, l], 1), side(qs[:], 1), side(Tl[:, l % 2, 0], 1), ALU.mult)
                    nc.vector.tensor_tensor(side(KL[:, l], 0), side(kk[:, 0], 0), side(Tl[:, l % 2, 0], 0), ALU.mult)
                    nc.vector.tensor_tensor(side(KL[:, l], 1), side(kk[:, 1], 1), side(Tl[:, l % 2, 1], 1),
                                            ALU.mult).then_inc(lv_ready, 1)
                    dve.wait_ge(lv_ready, i * (LEVELS + 1) + (l + 1))

                level_log(0)
                dve.wait_ge(ex_ready, i + 1)
                chain(nc.vector.tensor_copy(ed[:, 0], Xv[:, 0, :, P - 1]))
                chain(nc.vector.tensor_copy(ed[:, 1], Xv[:, 2, :, 0]))
                for n, (a, b) in enumerate(((qs[:], 0), (kk[:, 0], 1), (qs[:], 2), (kk[:, 1], 3))):
                    last = nc.vector.tensor_tensor(X[:, b], X[:, b], a, ALU.mult)
                last.then_inc(kd_ready, 1)
                for l in range(LEVELS):
                    if l + 1 < LEVELS:
                        level_log(l + 1)
                    level_scale(l)
                chain(nc.vector.tensor_copy(core.spare[:, 1:2], core.spare[:, 0:1]))
                dve.engine_nop().then_inc(lv_ready, 1)

                def merge(l):
                    dve.wait_ge(lvl_done, i * (LEVELS + 1) + (l + 1))
                    chain(nc.vector.tensor_copy(core.spare[:, 1:2], core.spare[:, 0:1]))
                    nc.vector.copy_predicated(A[:], masks[:, l].unsqueeze(1).to_broadcast([P, NB, P]),
                                              pA[:, l % 2].rearrange("p (n t) -> p n t", t=P)).then_inc(merged, 1)

                for l in range(3):
                    merge(l)
                dve.wait_ge(kv_done, i + 1)
                kv = pT[:].rearrange("p a c -> p (a c)")
                chain(nc.vector.tensor_copy(S[:, 0], kv[:, 0:P]))
                chain(nc.vector.scalar_tensor_tensor(out=S[:, 1], in0=S[:, 0], scalar=ed[:, 0, 1:2],
                                                     in1=kv[:, P:2 * P], op0=ALU.mult, op1=ALU.add))
                chain(nc.vector.scalar_tensor_tensor(out=S[:, 2], in0=S[:, 1], scalar=ed[:, 0, 2:3],
                                                     in1=kv[:, 2 * P:3 * P], op0=ALU.mult, op1=ALU.add))
                chain(nc.vector.tensor_copy(S[:, 5], kv[:, 5 * P:6 * P]))
                chain(nc.vector.scalar_tensor_tensor(out=S[:, 4], in0=S[:, 5], scalar=ed[:, 1, 2:3],
                                                     in1=kv[:, 4 * P:5 * P], op0=ALU.mult, op1=ALU.add))
                nc.vector.scalar_tensor_tensor(out=S[:, 3], in0=S[:, 4], scalar=ed[:, 1, 1:2],
                                               in1=kv[:, 3 * P:4 * P], op0=ALU.mult, op1=ALU.add).then_inc(st_ready, 1)
                for l in range(3, LEVELS + 1):
                    merge(l)
                dve.wait_ge(rs_done, i + 1)
                chain(nc.vector.scalar_tensor_tensor(out=sg[:], in0=pO[:], scalar=col(core, "gnorm"), in1=sg[:],
                                                     op0=ALU.mult, op1=ALU.mult))
                nc.vector.tensor_tensor(flat(yaT[:, bass.ds(h[0], 1)]), sg[:], rs[:], ALU.mult).then_inc(y_done, 1)
                dve.wait_ge(y_done, i + 2)
                chain(nc.vector.tensor_copy(core.spare[:, 1:2], core.spare[:, 0:1]))

            @block.vector
            def _(dve):
                chain = Chain(dve, dch)
                lb = core.cols[:, COLS["lb"]:COLS["lb"] + 16]
                nc.vector.tensor_tensor(lnf[:], lb, lb, ALU.subtract).then_inc(lbs, 1)
                dve.wait_ge(lbs, 2)
                chain(nc.vector.reciprocal(lnd[:], lnf[:]))
                chain(nc.vector.tensor_tensor(lnf[:], lnf[:], lnd[:], ALU.mult))
                chain(nc.vector.tensor_tensor(lnd[:], lnf[:], lnf[:], ALU.subtract))
                nc.vector.tensor_scalar(lnf[:], lnd[:], LB_FLOOR, None, ALU.max).then_inc(lbs, 1)
                dve.wait_ge(lbs, 5)
                nc.vector.tensor_scalar(lnf[:], lnf[:], -float(LN_SHIFT * np.log(2.0)), None, ALU.add).then_inc(lbs, 1)
                dve.wait_ge(lbs, 6)
                nc.vector.tensor_tensor(lnd[:], ln1[:], lnf[:], ALU.subtract).then_inc(lbs, 1)
                dve.wait_ge(lbs, 7)
                nc.vector.memset(A[:], 0.0).then_inc(merged, 2)
                nc.vector.memset(QL[:], 0.0).then_inc(st_ready, 1)
                nc.vector.memset(KL[:], 0.0).then_inc(y_done, 1)
                dve.wait_ge(merged, 2)
                dve.wait_ge(y_done, 1)
                dve.wait_ge(aux, 32)
                chain.restart()
                with dve.Fori(0, HEADS - 1) as i:
                    h = [dve.snap(i), dve.snap(i + HEADS)]
                    dve_head(dve, i, chain, h)
                    chain.restart()
                dve_head(dve, HEADS - 1, chain, [HEADS - 1, 2 * HEADS - 1])
    for j in range(QKV):
        core.w_n[j] += 16 * HEADS


def spatial_stage(core, ybT):
    nc, dram, hT = core.nc, core.dram, core.hT
    VS = 4
    with ExitStack() as ctx:
        def sb(name, shape):
            return ctx.enter_context(nc.sbuf_tensor("sg_" + name, shape, F32))

        vg = sb("v", [P, NB, D])
        lw, lbias = sb("ln_w", [P, D]), sb("ln_b", [P, D])
        junk = sb("junk", [P, D])
        st = sb("stats", [P, NB, 4])
        vst = sb("v_group", [P, 2, NB, P])
        ws = sb("w_s", [P, 2, P])
        bs = sb("b_s", [1, HEADS * P])
        ug, gg = sb("u", [P, 2, T]), sb("gate", [P, 2, T])
        pv = ctx.enter_context(nc.psum_tensor("sg_pv", [P, 2, 512], F32))
        pu = ctx.enter_context(nc.psum_tensor("sg_pu", [P, 2, 512], F32))
        pg = ctx.enter_context(nc.psum_tensor("sg_pg", [P, 2, 512], F32))
        pm = ctx.enter_context(nc.psum_tensor("sg_pm", [P, 2, 512], F32))
        aux, v_done, v_gelu, stat, norm = (core.sem(n) for n in ("aux", "v_done", "v_gelu", "stat", "norm"))
        ws_in = [core.sem("ws_in"), core.sem("ws_in")]
        u_done, g_done, m_done = (core.sem(n) for n in ("u_done", "gate_done", "mixed_done"))
        u_out, g_out, vst_ready, y_done = (core.sem(n) for n in ("u_out", "gate_out", "group_ready", "y_done"))
        dch = core.sem("dve_chain")
        w0 = list(core.w_n)
        with nc.Block() as block:
            @block.sync
            def _(sp):
                sp.dma_start(core.W[:, VS:VS + 8, :].rearrange("p s c -> p (s c)"), dram["w_v"][:])\
                    .then_inc(core.w_in[VS], 16)
                for j in range(4):
                    sp.dma_start(core.W[:, j, :], dram["w_ug"][0:1, :, j, :].rearrange("g p c -> p (g c)"))\
                        .then_inc(core.w_in[j], 16)
                sp.dma_start(lw[:], dram["ln_w"][0:1].partition_broadcast(P)).then_inc(aux, 16)
                sp.dma_start(lbias[:], dram["ln_b"][0:1].partition_broadcast(P)).then_inc(aux, 16)
                sp.dma_start(bs[:], dram["b_s"][:]).then_inc(aux, 16)
                for e in range(2):
                    sp.dma_start(ws[:, e], dram["w_s"][e]).then_inc(ws_in[e], 16)
                with sp.Fori(0, HEADS // 2 - 1) as i:
                    nxt = sp.snap(i + 1)
                    for e in range(2):
                        for j, used in ((2 * e, u_done), (2 * e + 1, g_done)):
                            src = dram["w_ug"][bass.ds(nxt, 1), :, j, :].rearrange("g p c -> p (g c)")
                            sp.wait_ge(used, i * 2 + (e + 1))
                            sp.dma_start(core.W[:, j, :], src).then_inc(core.w_in[j], 16)
                        src = dram["w_s"][bass.ds(sp.snap(i * 2 + (2 + e)), 1)].rearrange("g s t -> s (g t)")
                        sp.wait_ge(m_done, i * 2 + (e + 1))
                        sp.dma_start(ws[:, e], src).then_inc(ws_in[e], 16)

            def group(pe, i, e):
                for j, bank, done, out in ((2 * e, pu, u_done, u_out), (2 * e + 1, pg, g_done, g_out)):
                    pe.wait_ge(core.w_in[j], i * 16 + (w0[j] + 16))
                    pe.wait_ge(out, i * 2 + (e + 1))
                    for k in range(KT):
                        last = nc.tensor.matmul(bank[:, e, :], core.slot(j)[:, k, :], hT[:, k, :],
                                                start=(k == 0), stop=(k == KT - 1))
                    last.then_inc(done, 1)
                pe.wait_ge(vst_ready, i * 2 + (e + 1))
                pe.wait_ge(ws_in[e], i * 16 + 16)
                pe.wait_ge(y_done, i * 2 + (e + 1))
                for n in range(NB):
                    o = pm[:, e, n * P:(n + 1) * P]
                    nc.tensor.matmul(o, vst[:, e, n, :], ws[:, e, :], start=True, stop=False)
                    last = nc.tensor.matmul(o, core.ones[0:1, :], bsg[0:1, e, :], start=False, stop=True)
                last.then_inc(m_done, 1)

            bsg = ctx.enter_context(nc.sbuf_tensor("sg_bsg", [1, 2, P], F32))

            @block.tensor
            def _(pe):
                wv = core.wide(VS, 8, D)
                pe.wait_ge(core.w_in[VS], w0[VS] + 16)
                for n in range(NB):
                    for half in range(2):
                        m = 2 * n + half
                        if m >= 2:
                            pe.wait_ge(v_gelu, m - 1)
                        for k in range(KT):
                            last = nc.tensor.matmul(pv[:, half, :], hT[:, k, n * P:(n + 1) * P],
                                                    wv[:, k, half * 512:half * 512 + 512],
                                                    start=(k == 0), stop=(k == KT - 1))
                        last.then_inc(v_done, 1)
                with pe.Fori(0, HEADS // 2) as i:
                    for e in range(2):
                        group(pe, i, e)

            @block.scalar
            def _(act):
                for m in range(2 * NB):
                    act.wait_ge(v_done, m + 1)
                    nc.scalar.activation(vg[:, m // 2, (m % 2) * 512:(m % 2) * 512 + 512], pv[:, m % 2, :],
                                         ACT.Gelu_apprx_tanh).then_inc(v_gelu, 1)
                for n in range(NB):
                    act.wait_ge(stat, 2 * n + 1)
                    nc.scalar.activation(junk[:], vg[:, n], ACT.Square, bias=st[:, n, 1:2],
                                         accum_out=st[:, n, 2:3]).then_inc(norm, 1)
                    act.wait_ge(norm, n + 1)
                act.wait_ge(stat, 2 * NB)
                nc.scalar.activation(st[:, :, 2], st[:, :, 2], ACT.Sqrt, bias=core.eps[:, 1:2],
                                     scale=1.0 / D).then_inc(norm, 1)
                with act.Fori(0, HEADS // 2) as i:
                    for e in range(2):
                        act.wait_ge(u_done, i * 2 + (e + 1))
                        act.wait_ge(y_done, i * 2 + (e + 1))
                        nc.scalar.activation(ug[:, e], pu[:, e, :], ACT.Gelu_apprx_tanh).then_inc(u_out, 1)
                    for e in range(2):
                        act.wait_ge(g_done, i * 2 + (e + 1))
                        nc.scalar.activation(gg[:, e], pg[:, e, :], ACT.Silu).then_inc(g_out, 1)

            @block.vector
            def _(dve):
                chain = Chain(dve, dch)
                for n in range(NB):
                    dve.wait_ge(v_gelu, 2 * n + 2)
                    chain(nc.vector.tensor_reduce(st[:, n, 0:1], vg[:, n], AX_X, ALU.add))
                    nc.vector.tensor_scalar(st[:, n, 1:2], st[:, n, 0:1], -1.0 / D, None, ALU.mult).then_inc(stat, 1)
                    dve.wait_ge(stat, 2 * n + 1)
                    chain(nc.vector.tensor_copy(core.spare[:, 1:2], core.spare[:, 0:1]))
                    dve.engine_nop().then_inc(stat, 1)
                dve.wait_ge(norm, NB + 1)
                chain(nc.vector.reciprocal(st[:, :, 0], st[:, :, 2]))
                dve.wait_ge(aux, 48)
                for n in range(NB):
                    chain(nc.vector.tensor_scalar(vg[:, n], vg[:, n], st[:, n, 1:2], st[:, n, 0:1], ALU.add, ALU.mult))
                    chain(nc.vector.tensor_tensor(vg[:, n], vg[:, n], lw[:], ALU.mult))
                    chain(nc.vector.tensor_tensor(vg[:, n], vg[:, n], lbias[:], ALU.add))
                nc.vector.memset(st[:, 0, 0:1], 0.0).then_inc(u_out, 2)
                nc.vector.memset(st[:, 1, 0:1], 0.0).then_inc(g_out, 2)
                nc.vector.memset(st[:, 2, 0:1], 0.0).then_inc(y_done, 2)
                chain.restart()
                with dve.Fori(0, HEADS // 2) as i:
                    for e in range(2):
                        g = dve.snap(i * 2 + e)
                        dve.wait_ge(y_done, i * 2 + (e + 1))
                        nc.vector.tensor_copy(bsg[0:1, e, :], bs[0:1, bass.ds(g * P, P)])
                        nc.vector.tensor_copy(vst[:, e], vg[:, :, bass.ds(g * P, P)]).then_inc(vst_ready, 1)
                    for e in range(2):
                        g = dve.snap(i * 2 + e)
                        dve.wait_ge(g_out, i * 2 + (e + 3))
                        dve.wait_ge(m_done, i * 2 + (e + 1))
                        chain(nc.vector.tensor_tensor(ug[:, e], ug[:, e], pm[:, e, :], ALU.mult))
                        nc.vector.tensor_tensor(flat(ybT[:, bass.ds(g, 1)]), ug[:, e], gg[:, e],
                                                ALU.mult).then_inc(y_done, 1)
                    chain(nc.vector.tensor_copy(core.spare[:, 1:2], core.spare[:, 0:1]))
                    chain.restart()
        for j in range(4):
            core.w_n[j] += 16 * (HEADS // 2)
        core.w_n[VS] += 16


def merge_stage(core, yaT, ybT, mT):
    nc, dram = core.nc, core.dram
    acts = (core.hT, yaT, core.hT, ybT)
    with (nc.sbuf_tensor("mg_sig", [P, 2, T], F32) as sig, nc.psum_tensor("mg_p", [P, 2, 4, 512], F32) as pp,
          nc.Block() as block):
        done = [core.sem(f"merge_{n}") for n in ("ma", "pa", "mb", "pb")]
        sig_done, out_done, dch = core.sem("sig_done"), core.sem("merged"), core.sem("dve_chain")
        w0 = list(core.w_n)

        @block.sync
        def _(sp):
            for j in range(4):
                sp.dma_start(core.W[:, j, :], dram["w_merge"][0:1, :, j, :].rearrange("d p c -> p (d c)"))\
                    .then_inc(core.w_in[j], 16)
            with sp.Fori(0, KT - 1) as i:
                nxt = sp.snap(i + 1)
                for j in range(4):
                    src = dram["w_merge"][bass.ds(nxt, 1), :, j, :].rearrange("d p c -> p (d c)")
                    sp.wait_ge(done[j], i + 1)
                    sp.dma_start(core.W[:, j, :], src).then_inc(core.w_in[j], 16)

        @block.tensor
        def _(pe):
            with pe.Fori(0, KT) as i:
                for j in range(4):
                    pe.wait_ge(core.w_in[j], i * 16 + (w0[j] + 16))
                    pe.wait_ge(out_done, i + 1)
                    for k in range(KT):
                        last = nc.tensor.matmul(pp[:, 0, j, :], core.slot(j)[:, k, :], acts[j][:, k, :],
                                                start=(k == 0), stop=(k == KT - 1))
                    last.then_inc(done[j], 1)

        @block.scalar
        def _(act):
            with act.Fori(0, KT) as i:
                for n, j in enumerate((0, 2)):
                    act.wait_ge(done[j], i + 1)
                    act.wait_ge(out_done, i + 1)
                    nc.scalar.activation(sig[:, n], pp[:, 0, j, :], ACT.Sigmoid).then_inc(sig_done, 1)

        @block.vector
        def _(dve):
            chain = Chain(dve, dch)
            nc.vector.memset(mT[:, 0, 0:1], 0.0).then_inc(out_done, 1)
            dve.wait_ge(out_done, 1)
            with dve.Fori(0, KT) as i:
                o = flat(mT[:, bass.ds(dve.snap(i), 1)])
                for n, j in enumerate((1, 3)):
                    dve.wait_ge(sig_done, i * 2 + (n + 1))
                    dve.wait_ge(done[j], i + 1)
                    chain(nc.vector.tensor_tensor(sig[:, n], sig[:, n], pp[:, 0, j, :], ALU.mult))
                nc.vector.tensor_tensor(o, sig[:, 0], sig[:, 1], ALU.add).then_inc(out_done, 1)
                dve.wait_ge(out_done, i + 2)
                chain(nc.vector.tensor_copy(core.spare[:, 1:2], core.spare[:, 0:1]))
                chain.restart()
    for j in range(4):
        core.w_n[j] += 16 * KT


def residual_stage(core, name, kt, src):
    nc, dram = core.nc, core.dram
    w = dram[name]
    J = 4
    with nc.psum_tensor(name + "_p", [P, J, 512], F32) as pp, nc.Block() as block:
        done, added = [core.sem("proj") for _ in range(J)], core.sem("added")
        w0 = list(core.w_n)
        turns = KT // J

        @block.sync
        def _(sp):
            for j in range(J):
                sp.dma_start(core.W[:, j, 0:kt * P], w[j]).then_inc(core.w_in[j], 16)
            for j in range(J):
                sp.wait_ge(done[j], 1)
                sp.dma_start(core.W[:, j, 0:kt * P], w[J + j]).then_inc(core.w_in[j], 16)

        @block.tensor
        def _(pe):
            for i in range(turns):
                for j in range(J):
                    pe.wait_ge(core.w_in[j], w0[j] + 16 * (i + 1))
                    if i:
                        pe.wait_ge(added, J * (i - 1) + j + 1)
                    for k in range(kt):
                        last = nc.tensor.matmul(pp[:, j, :], core.slot(j)[:, k, :], src[:, k, :],
                                                start=(k == 0), stop=(k == kt - 1))
                    last.then_inc(done[j], 1)

        @block.vector
        def _(dve):
            for i in range(turns):
                for j in range(J):
                    dve.wait_ge(done[j], i + 1)
                    x = core.xT[:, J * i + j]
                    nc.vector.tensor_tensor(x, x, pp[:, j, :], ALU.add).then_inc(added, 1)
    for j in range(J):
        core.w_n[j] += 16 * turns


def rope_stage(core, name, tiles, norm, dst, first, J):
    nc, dram, hT = core.nc, core.dram, core.hT
    turns = tiles // J
    with ExitStack() as ctx:
        def sb(n, shape):
            return ctx.enter_context(nc.sbuf_tensor(f"rope_{n}{core.names}", shape, F32))

        def ps(n):
            return ctx.enter_context(nc.psum_tensor(f"rope_{n}{core.names}", [P, J, 512], F32))
        sq, rs, zn, tm = sb("sq", [P, J, T]), sb("rs", [P, J, T]), sb("zn", [P, J, T]), sb("tm", [P, J, T])
        pz, pss, pr = ps("pz"), ps("ps"), ps("pr")
        z_done, sq_done, ss_done, rs_done, zn_done, rot_done, out_done, dch, ach = (core.sem(n) for n in (
            "z_done", "sq_done", "ss_done", "rs_done", "zn_done", "rot_done", "rope_out", "dve_chain", "act_chain"))
        w0 = list(core.w_n)
        w = dram[name]
        with nc.Block() as block:
            @block.sync
            def _(sp):
                for j in range(J):
                    sp.dma_start(core.W[:, j, :], w[j]).then_inc(core.w_in[j], 16)
                if turns > 1:
                    with sp.Fori(0, turns - 1) as i:
                        for j in range(J):
                            src = w[bass.ds(sp.snap(i * J + (J + j)), 1)].rearrange("d p c -> p (d c)")
                            sp.wait_ge(z_done, i * J + (j + 1))
                            sp.dma_start(core.W[:, j, :], src).then_inc(core.w_in[j], 16)

            @block.tensor
            def _(pe):
                with pe.Fori(0, turns) as i:
                    for j in range(J):
                        pe.wait_ge(core.w_in[j], i * 16 + (w0[j] + 16))
                        pe.wait_ge(out_done, i * J + (j + 1))
                        for k in range(KT):
                            last = nc.tensor.matmul(pz[:, j, :], core.slot(j)[:, k, :], hT[:, k, :],
                                                    start=(k == 0), stop=(k == KT - 1))
                        last.then_inc(z_done, 1)
                    for j in range(J if norm else 0):
                        pe.wait_ge(sq_done, i * J + (j + 1))
                        nc.tensor.matmul(pss[:, j, :], core.pair_ones[:], sq[:, j], start=True,
                                         stop=True).then_inc(ss_done, 1)
                    for j in range(J):
                        pe.wait_ge(zn_done, i * J + (j + 1))
                        nc.tensor.matmul(pr[:, j, :], core.rot[:], zn[:, j], start=True,
                                         stop=True).then_inc(rot_done, 1)

            @block.scalar
            def _(act):
                chain = Chain(act, ach)
                if norm:
                    with act.Fori(0, turns) as i:
                        for j in range(J):
                            act.wait_ge(z_done, i * J + (j + 1))
                            nc.scalar.activation(sq[:, j], pz[:, j, :], ACT.Square).then_inc(sq_done, 1)
                        for j in range(J):
                            act.wait_ge(ss_done, i * J + (j + 1))
                            act.wait_ge(out_done, i * J + (J if turns > 1 else j + 1))
                            chain(nc.scalar.activation(rs[:, j], pss[:, j, :], ACT.Ln, bias=core.eps[:, 0:1],
                                                       scale=2.0 / P))
                            nc.scalar.activation(rs[:, j], rs[:, j], ACT.Exp, scale=-0.5).then_inc(rs_done, 1)
                        chain.restart()

            @block.vector
            def _(dve):
                chain = Chain(dve, dch)
                nc.vector.memset(zn[:, 0, 0:1], 0.0).then_inc(out_done, J)
                dve.wait_ge(out_done, J)
                with dve.Fori(0, turns) as i:
                    for j in range(J):
                        if norm:
                            dve.wait_ge(rs_done, i * J + (j + 1))
                            ins = nc.vector.scalar_tensor_tensor(out=zn[:, j], in0=pz[:, j, :], scalar=col(core, norm),
                                                                 in1=rs[:, j], op0=ALU.mult, op1=ALU.mult)
                        else:
                            dve.wait_ge(z_done, i * J + (j + 1))
                            ins = nc.vector.tensor_copy(zn[:, j], pz[:, j, :])
                        ins.then_inc(zn_done, 1)
                    for j in range(J):
                        o = flat(dst[:, bass.ds(dve.snap(i * J + (first + j)), 1)])
                        dve.wait_ge(zn_done, i * J + (j + 1))
                        chain(nc.vector.tensor_tensor(tm[:, j], zn[:, j], core.cos[:], ALU.mult))
                        dve.wait_ge(rot_done, i * J + (j + 1))
                        chain(nc.vector.tensor_tensor(zn[:, j], pr[:, j, :], core.sin[:], ALU.mult))
                        nc.vector.tensor_tensor(o, tm[:, j], zn[:, j], ALU.add).then_inc(out_done, 1)
                    dve.wait_ge(out_done, i * J + 2 * J)
                    chain(nc.vector.tensor_copy(core.spare[:, 1:2], core.spare[:, 0:1]))
                    chain.restart()
    for j in range(J):
        core.w_n[j] += 16 * turns


def natural_stage(core, name, src, kt, rows, cols, dst):
    nc, dram = core.nc, core.dram
    slots = -(-kt * cols // (KT * P))
    w = core.wide(0, slots, cols) if kt * cols == slots * KT * P else \
        core.W[:, 0, 0:kt * cols].rearrange("p (k c) -> p k c", c=cols)
    with nc.psum_tensor(f"nat{core.names}", [P, 2, 512], F32) as pp, nc.Block() as block:
        done, out = core.sem("natural_done"), core.sem("natural_out")
        w0 = core.w_n[0]

        @block.sync
        def _(sp):
            sp.dma_start(w, dram[name].rearrange("p (k c) -> p k c", c=cols)).then_inc(core.w_in[0], 16)

        @block.tensor
        def _(pe):
            pe.wait_ge(core.w_in[0], w0 + 16)
            for n in range(rows):
                if n >= 2:
                    pe.wait_ge(out, n - 1)
                for k in range(kt):
                    last = nc.tensor.matmul(pp[:, n % 2, 0:cols], src[:, k, n * P:(n + 1) * P], w[:, k, :],
                                            start=(k == 0), stop=(k == kt - 1))
                last.then_inc(done, 1)

        @block.scalar
        def _(act):
            for n in range(rows):
                act.wait_ge(done, n + 1)
                nc.scalar.copy(dst[:, n], pp[:, n % 2, 0:cols]).then_inc(out, 1)
    core.w_n[0] += 16


def turn_stage(core, src, n_in, n_out, dst, d0):
    nc = core.nc
    with nc.psum_tensor(f"turn{core.names}", [P, 2, 512], F32) as pp, nc.Block() as block:
        done, out = core.sem("turned"), core.sem("turned_out")

        @block.tensor
        def _(pe):
            for o in range(n_out):
                if o >= 2:
                    pe.wait_ge(out, o - 1)
                for i in range(n_in):
                    last = nc.tensor.transpose(pp[:, o % 2, i * P:(i + 1) * P], src[:, i, o * P:(o + 1) * P],
                                               core.ident[:])
                last.then_inc(done, 1)

        @block.scalar
        def _(act):
            for o in range(n_out):
                act.wait_ge(done, o + 1)
                nc.scalar.copy(dst[:, d0 + o, 0:n_in * P], pp[:, o % 2, 0:n_in * P]).then_inc(out, 1)


def pool_stage(core, yT):
    nc, dram, hT = core.nc, core.dram, core.hT
    PAD = 16
    with ExitStack() as ctx:
        def sb(n, shape):
            return ctx.enter_context(nc.sbuf_tensor("pool_" + n, shape, F32))
        u = sb("u", [P, 4, PAD + T])
        s = sb("s", [P, 4, 2, PAD + T])
        mx = sb("mixed", [P, 4, T])
        inv, small, pw = sb("inv", [P, 4, PAD]), sb("small", [P, 4, PAD]), sb("w", [P, 4, P])
        pz = ctx.enter_context(nc.psum_tensor("pool_z", [P, 4, 512], F32))
        pm = ctx.enter_context(nc.psum_tensor("pool_m", [P, 4, 512], F32))
        aux, zdone, uready, mready, mdone, zero, dch = (core.sem(n) for n in (
            "aux", "pool_z", "pool_u", "pool_mixed", "pool_done", "pad_zero", "dve_chain"))
        w0 = list(core.w_n)
        with nc.Block() as block:
            @block.sync
            def _(sp):
                for j in range(4):
                    sp.dma_start(core.W[:, j, :], dram["w_pool_in"][j]).then_inc(core.w_in[j], 16)
                sp.dma_start(inv[:], dram["pool_inv"][:]).then_inc(aux, 16)
                sp.dma_start(pw[:], dram["pool_w"][:]).then_inc(aux, 16)

            @block.tensor
            def _(pe):
                for g in range(4):
                    pe.wait_ge(core.w_in[g], w0[g] + 16)
                    for k in range(KT):
                        last = nc.tensor.matmul(pz[:, g, :], core.slot(g)[:, k, :], hT[:, k, :],
                                                start=(k == 0), stop=(k == KT - 1))
                    last.then_inc(zdone, 1)
                pe.wait_ge(aux, 32)
                for g in range(4):
                    pe.wait_ge(mready, g + 1)
                    nc.tensor.matmul(pm[:, g, :], pw[:, g, :], mx[:, g], start=True, stop=True).then_inc(mdone, 1)

            @block.scalar
            def _(act):
                for g in range(4):
                    act.wait_ge(zdone, g + 1)
                    nc.scalar.copy(u[:, g, PAD:], pz[:, g, :]).then_inc(uready, 1)

            @block.vector
            def _(dve):
                chain = Chain(dve, dch)
                chain(nc.vector.memset(u[:, :, 0:PAD], 0.0))
                chain(nc.vector.memset(s[:, :, :, 0:PAD], 0.0))
                dve.wait_ge(aux, 32)
                for g in range(4):
                    dve.wait_ge(uready, g + 1)
                    cur = u[:, g]
                    for n in range(g + 1):
                        o = s[:, g, n % 2]
                        chain(nc.vector.tensor_tensor(o[:, PAD:], cur[:, PAD:], cur[:, PAD - 2 ** n:PAD + T - 2 ** n],
                                                      ALU.add))
                        cur = o
                    chain(nc.vector.scalar_tensor_tensor(out=mx[:, g], in0=cur[:, PAD:], scalar=1.0 / 2 ** (g + 1),
                                                         in1=u[:, g, PAD:], op0=ALU.mult, op1=ALU.subtract))
                    chain(nc.vector.tensor_tensor(small[:, g], cur[:, PAD:2 * PAD], inv[:, g], ALU.mult))
                    nc.vector.tensor_tensor(mx[:, g, 0:PAD], small[:, g], u[:, g, PAD:2 * PAD],
                                            ALU.subtract).then_inc(mready, 1)
                for g in range(4):
                    dve.wait_ge(mdone, g + 1)
                    nc.vector.tensor_scalar(yT[:, g], pm[:, g, :], col(core, "pool_scale", g), None, ALU.mult)
    for j in range(4):
        core.w_n[j] += 16


def index_stage(core, qiT, kiT, wi, bias):
    nc, dram = core.nc, core.dram
    IH = 8
    with ExitStack() as ctx:
        def sb(n, shape):
            return ctx.enter_context(nc.sbuf_tensor("idx_" + n, shape, F32))
        rel = sb("rel", [P, 3, T])
        acc = sb("acc", [P, 3, T])
        best = sb("best", [P, 3, 8])
        hide = sb("hide", [P, P])
        pp = ctx.enter_context(nc.psum_tensor("idx_p", [P, 4, 512], F32))
        done, relu, used, aux, dch = (core.sem(n) for n in ("idx_done", "relu", "rel_used", "aux", "dve_chain"))
        units = [(b, h) for b in (3, 2, 1) for h in range(IH)]
        with nc.Block() as block:
            @block.sync
            def _(sp):
                sp.dma_start(hide[:], dram["hide"][:]).then_inc(aux, 16)

            @block.tensor
            def _(pe):
                for u, (b, h) in enumerate(units):
                    r = slice(64 * (h % 2), 64 * (h % 2) + 64)
                    if u >= 4:
                        pe.wait_ge(relu, u - 3)
                    nc.tensor.matmul(pp[:, u % 4, 0:(b + 1) * P], qiT[r, h // 2, b * P:(b + 1) * P],
                                     kiT[r, 0, 0:(b + 1) * P], start=True, stop=True).then_inc(done, 1)

            @block.scalar
            def _(act):
                for u, (b, h) in enumerate(units):
                    act.wait_ge(done, u + 1)
                    if u >= 3:
                        act.wait_ge(used, u - 2)
                    w = (b + 1) * P
                    nc.scalar.activation(rel[:, u % 3, 0:w], pp[:, u % 4, 0:w], ACT.Relu).then_inc(relu, 1)

            @block.vector
            def _(dve):
                chain = Chain(dve, dch)
                chain(nc.vector.tensor_scalar(wi[:], wi[:], (64 ** -0.5) * (IH ** -0.5), None, ALU.mult))
                dve.wait_ge(aux, 16)
                for u, (b, h) in enumerate(units):
                    w = (b + 1) * P
                    a = acc[:, b - 1, 0:w]
                    dve.wait_ge(relu, u + 1)
                    if h == 0:
                        nc.vector.tensor_scalar(a, rel[:, u % 3, 0:w], wi[:, b, h:h + 1], None,
                                                ALU.mult).then_inc(used, 1)
                    else:
                        nc.vector.scalar_tensor_tensor(out=a, in0=rel[:, u % 3, 0:w], scalar=wi[:, b, h:h + 1], in1=a,
                                                       op0=ALU.mult, op1=ALU.add).then_inc(used, 1)
                    dve.wait_ge(used, u + 1)
                nc.vector.tensor_scalar(bias[:, 0, 0:P], hide[:], MASKED / HIDDEN, None, ALU.mult)
                for b in (1, 2, 3):
                    chain(nc.vector.tensor_tensor(acc[:, b - 1, b * P:(b + 1) * P], acc[:, b - 1, b * P:(b + 1) * P],
                                                  hide[:], ALU.add))
                for r in range(SEL // 8):
                    for b in (1, 2, 3):
                        a = acc[:, b - 1, 0:(b + 1) * P]
                        chain(nc.vector.max(best[:, b - 1], a))
                        chain(nc.vector.match_replace(a, best[:, b - 1], a, REPLACED))
                for b in (1, 2, 3):
                    w = (b + 1) * P
                    nc.vector.tensor_scalar(bias[:, b, 0:w], acc[:, b - 1, 0:w], 0.5 * (REPLACED + HIDDEN), MASKED,
                                            ALU.is_gt, ALU.mult)


def attention_stage(core, name, qT, kT, v, y, tiles, dh, scale, widths, bias):
    nc = core.nc
    U = (P // dh) * NB
    units = [(hh, b) for hh in range(P // dh) for b in range(NB)]
    with ExitStack() as ctx:
        def sb(n, shape):
            return ctx.enter_context(nc.sbuf_tensor(name + n, shape, F32))

        def ps(n):
            return ctx.enter_context(nc.psum_tensor(name + n, [P, 2, 512], F32))
        kw = max(widths)
        q1, k1 = sb("q1", [P, T]), sb("k1", [P, kw])
        pr, prT = sb("probs", [P, 2, kw]), sb("probsT", [P, 2, kw])
        nm, sm, rc = sb("negmax", [P, U]), sb("sum", [P, U]), sb("rec", [P, U])
        pS, pT, pO = ps("S"), ps("T"), ps("O")
        qk, s_done, nm_done, p_done, t_done, t_out, o_done, y_out, dch = (core.sem(name + n) for n in (
            "qk", "s_done", "negmax", "probs", "turned", "turned_out", "o_done", "y_out", "dve_chain"))
        with nc.Block() as block:
            @block.tensor
            def _(pe):
                def scores(i, u):
                    hh, b = units[u]
                    r = slice(hh * dh, hh * dh + dh)
                    w = widths[b]
                    pe.wait_ge(p_done, i * U + (u + 1))
                    nc.tensor.matmul(pS[:, u % 2, 0:w], q1[r, b * P:(b + 1) * P], k1[r, 0:w], start=True,
                                     stop=True).then_inc(s_done, 1)

                def turn(i, u):
                    w = widths[units[u][1]]
                    pe.wait_ge(p_done, i * U + (u + 3))
                    pe.wait_ge(t_out, i * U + (u + 1))
                    for c in range(w // P):
                        last = nc.tensor.transpose(pT[:, u % 2, c * P:(c + 1) * P], pr[:, u % 2, c * P:(c + 1) * P],
                                                   core.ident[:])
                    last.then_inc(t_done, 1)

                def values(i, u, vcol):
                    hh, b = units[u]
                    n = widths[b] // P
                    pe.wait_ge(t_out, i * U + (u + 3))
                    pe.wait_ge(y_out, i * U + (u + 1))
                    for c in range(n):
                        last = nc.tensor.matmul(pO[:, u % 2, 0:dh], prT[:, u % 2, c * P:(c + 1) * P],
                                                v[:, c, bass.ds(vcol[hh], dh)], start=(c == 0), stop=(c == n - 1))
                    last.then_inc(o_done, 1)

                with pe.Fori(0, tiles) as i:
                    vcol = [pe.snap(i * P + hh * dh) for hh in range(P // dh)]
                    pe.wait_ge(qk, i + 1)
                    scores(i, 0)
                    for u in range(U):
                        if u + 1 < U:
                            scores(i, u + 1)
                        turn(i, u)
                        if u >= 1:
                            values(i, u - 1, vcol)
                    values(i, U - 1, vcol)

            @block.scalar
            def _(act):
                def expo(i, u):
                    w = widths[units[u][1]]
                    act.wait_ge(nm_done, i * U + (u + 1))
                    act.wait_ge(t_done, i * U + (u + 1))
                    src = pr[:, u % 2, 0:w] if bias is not None else pS[:, u % 2, 0:w]
                    nc.scalar.activation(pr[:, u % 2, 0:w], src, ACT.Exp, bias=nm[:, u:u + 1],
                                         accum_out=sm[:, u:u + 1]).then_inc(p_done, 1)

                def copy(i, u):
                    w = widths[units[u][1]]
                    act.wait_ge(t_done, i * U + (u + 3))
                    act.wait_ge(o_done, i * U + (u + 1))
                    nc.scalar.copy(prT[:, u % 2, 0:w], pT[:, u % 2, 0:w]).then_inc(t_out, 1)

                with act.Fori(0, tiles) as i:
                    expo(i, 0)
                    for u in range(U):
                        if u + 1 < U:
                            expo(i, u + 1)
                        copy(i, u)

            @block.vector
            def _(dve):
                chain = Chain(dve, dch)

                def top(i, u):
                    w = widths[units[u][1]]
                    dve.wait_ge(s_done, i * U + (u + 1))
                    if bias is not None:
                        dve.wait_ge(t_done, i * U + (u + 1))
                        chain(nc.vector.tensor_copy(core.spare[:, 1:2], core.spare[:, 0:1]))
                        chain(nc.vector.tensor_tensor_reduce(pr[:, u % 2, 0:w], pS[:, u % 2, 0:w],
                                                             bias[:, units[u][1], 0:w], 1.0, -3.0e38, ALU.add, ALU.max,
                                                             rc[:, u:u + 1]))
                    else:
                        chain(nc.vector.tensor_reduce(rc[:, u:u + 1], pS[:, u % 2, 0:w], AX_X, ALU.max))
                    nc.vector.tensor_scalar(nm[:, u:u + 1], rc[:, u:u + 1], -1.0, None, ALU.mult).then_inc(nm_done, 1)

                def store(i, u, ycol):
                    hh, b = units[u]
                    dve.wait_ge(o_done, i * U + (u + 3))
                    chain(nc.vector.reciprocal(rc[:, u:u + 1], sm[:, u:u + 1]))
                    nc.vector.tensor_scalar(y[:, b, bass.ds(ycol[hh], dh)], pO[:, u % 2, 0:dh], rc[:, u:u + 1], None,
                                            ALU.mult).then_inc(y_out, 1)

                for n, s in enumerate((p_done, t_done, t_out, o_done, y_out)):
                    chain(nc.vector.tensor_copy(core.spare[:, 1:2], core.spare[:, 0:1]))
                    dve.engine_nop().then_inc(s, 2)
                chain.restart()
                with dve.Fori(0, tiles) as i:
                    at = dve.snap(i)
                    ycol = [dve.snap(i * P + hh * dh) for hh in range(P // dh)]
                    dve.wait_ge(o_done, i * U + 2)
                    nc.vector.tensor_scalar(q1[:], flat(qT[:, bass.ds(at, 1)]), scale, None, ALU.mult)
                    nc.vector.tensor_copy(k1[:], flat(kT[:, bass.ds(at, 1), 0:kw])).then_inc(qk, 1)
                    top(i, 0)
                    top(i, 1)
                    for u in range(U):
                        if u + 2 < U:
                            top(i, u + 2)
                        store(i, u, ycol)
                    chain.restart()


def norm_heads_stage(core, src, n, cols, weight):
    nc = core.nc
    with ExitStack() as ctx:
        sq = ctx.enter_context(nc.sbuf_tensor(f"nh_sq{core.names}", [P, n, cols], F32))
        rs = ctx.enter_context(nc.sbuf_tensor(f"nh_rs{core.names}", [P, n, cols], F32))
        pp = ctx.enter_context(nc.psum_tensor(f"nh_p{core.names}", [P, n, 512], F32))
        sq_done, ss_done, rs_done, ach = (core.sem(m) for m in ("sq", "ss", "rs", "act_chain"))
        with nc.Block() as block:
            @block.scalar
            def _(act):
                chain = Chain(act, ach)
                for k in range(n):
                    nc.scalar.activation(sq[:, k], src[:, k], ACT.Square).then_inc(sq_done, 1)
                for k in range(n):
                    act.wait_ge(ss_done, k + 1)
                    chain(nc.scalar.activation(rs[:, k], pp[:, k, 0:cols], ACT.Ln, bias=core.eps[:, 0:1],
                                               scale=1.0 / P))
                    nc.scalar.activation(rs[:, k], rs[:, k], ACT.Exp, scale=-0.5).then_inc(rs_done, 1)

            @block.tensor
            def _(pe):
                for k in range(n):
                    pe.wait_ge(sq_done, k + 1)
                    nc.tensor.matmul(pp[:, k, 0:cols], core.ones[:], sq[:, k], start=True, stop=True)\
                        .then_inc(ss_done, 1)

            @block.vector
            def _(dve):
                for k in range(n):
                    dve.wait_ge(rs_done, k + 1)
                    nc.vector.scalar_tensor_tensor(out=src[:, k], in0=src[:, k], scalar=col(core, weight),
                                                   in1=rs[:, k], op0=ALU.mult, op1=ALU.mult)


def project_stage(core, name, src, kt, n, cols, dst):
    nc, dram = core.nc, core.dram
    with nc.psum_tensor(f"pj{core.names}", [P, n, 512], F32) as pp, nc.Block() as block:
        done = core.sem("proj_done")
        w0 = list(core.w_n)

        @block.sync
        def _(sp):
            for j in range(n):
                sp.dma_start(core.W[:, j, 0:kt * P], dram[name][j]).then_inc(core.w_in[j], 16)

        @block.tensor
        def _(pe):
            for j in range(n):
                pe.wait_ge(core.w_in[j], w0[j] + 16)
                for k in range(kt):
                    last = nc.tensor.matmul(pp[:, j, 0:cols], core.slot(j)[:, k, :], src[:, k, 0:cols],
                                            start=(k == 0), stop=(k == kt - 1))
                last.then_inc(done, 1)

        @block.scalar
        def _(act):
            for j in range(n):
                act.wait_ge(done, j + 1)
                nc.scalar.copy(dst[:, j, 0:cols], pp[:, j, 0:cols])
    for j in range(n):
        core.w_n[j] += 16


def rows_stage(core, src, dst):
    nc = core.nc
    with nc.psum_tensor(f"rows{core.names}", [P, 2, 2, 512], F32) as pp, nc.Block() as block:
        done, out_a, out_b = core.sem("turned"), core.sem("turned_out_a"), core.sem("turned_out_b")

        @block.tensor
        def _(pe):
            for n in range(NB):
                if n >= 2:
                    pe.wait_ge(out_a, n - 1)
                    pe.wait_ge(out_b, n - 1)
                for k in range(KT):
                    last = nc.tensor.transpose(pp[:, n % 2, k // 4, (k % 4) * P:(k % 4 + 1) * P],
                                               src[:, k, n * P:(n + 1) * P], core.ident[:])
                last.then_inc(done, 1)

        @block.scalar
        def _(act):
            for n in range(NB):
                act.wait_ge(done, n + 1)
                nc.scalar.copy(dst[:, n, 0:512], pp[:, n % 2, 0, :]).then_inc(out_a, 1)

        @block.vector
        def _(dve):
            for n in range(NB):
                dve.wait_ge(done, n + 1)
                nc.vector.tensor_copy(dst[:, n, 512:1024], pp[:, n % 2, 1, :]).then_inc(out_b, 1)


def route_stage(core, logits, gate, pos, most, ix):
    nc, dram = core.nc, core.dram
    G = EXPERTS // EPG
    with ExitStack() as ctx:
        def sb(n, shape, dt=F32):
            return ctx.enter_context(nc.sbuf_tensor("rt_" + n, shape, dt))
        br, desc, eoff, ids = sb("bias", [P, 36]), sb("desc", [P, 32]), sb("eoff", [P, 32]), sb("ids", [P, NB])
        before = sb("before", [P, P])
        zero = sb("zero", [P, P + 1])
        gx, gk, go = sb("gx", [P, NB, G]), sb("gk", [P, NB, G]), sb("go", [P, NB, G])
        em, ek, o1, o2, A = (sb(n, [P, NB, EXPERTS]) for n in ("em", "ek", "o1", "o2", "A"))
        rk, rr = sb("rank", [P, NB, EXPERTS]), sb("round", [P, NB, EXPERTS])
        m = sb("m", [P, 8, NB])
        posf = sb("posf", [P, 2 * NB])
        li = sb("list", [P, P])
        pR = ctx.enter_context(nc.psum_tensor("rt_p_before", [P, NB, EXPERTS], F32))
        pC = ctx.enter_context(nc.psum_tensor("rt_p_count", [P, 512], F32))
        pL = ctx.enter_context(nc.psum_tensor("rt_p_turned", [P, 512], F32))
        aux, zeroed, expo, chosen, ranked, placed, listed, back, turned, dch, ach = (core.sem(n) for n in (
            "aux", "list_zeroed", "exp", "chosen", "ranked", "placed", "listed", "list_back", "turned", "dve_chain",
            "act_chain"))

        with nc.Block() as block:
            @block.sync
            def _(sp):
                sp.dma_start(br[:], dram["router_b"][0:1].partition_broadcast(P)).then_inc(aux, 16)
                sp.dma_start(desc[:], dram["moe_table"][:, 0:32]).then_inc(aux, 16)
                sp.dma_start(eoff[:], dram["moe_table"][:, 32:64]).then_inc(aux, 16)
                sp.dma_start(ids[:], dram["moe_table"][:, 64:64 + NB]).then_inc(aux, 16)
                sp.dma_start(before[:], dram["before"][:]).then_inc(aux, 16)
                sp.wait_ge(zeroed, 1)
                sp.dma_start(core.list.rearrange("(p f) o -> p (f o)", p=P), zero[:]).then_inc(aux, 16)
                sp.wait_ge(listed, 16 * 2 * NB)
                sp.dma_start(li[:], core.list[0:P * P].rearrange("(u j) o -> u (j o)", j=P)).then_inc(back, 16)

            @block.gpsimd
            def _(pool):
                pool.wait_ge(aux, 96)
                pool.wait_ge(placed, 1)
                for j in range(2 * NB):
                    nc.gpsimd.indirect_dma_start(
                        out=core.list[:], out_offset=bass.IndirectOffsetOnAxis(ap=pos[:, j:j + 1], axis=0),
                        in_=ids[:, j % NB:j % NB + 1], in_offset=None).then_inc(listed, 16)

            @block.scalar
            def _(act):
                act.wait_ge(expo, 1)
                nc.scalar.activation(gx[:], gx[:], ACT.Exp).then_inc(expo, 1)
                act.wait_ge(expo, 3)
                nc.scalar.activation(m[:, 5], m[:, 5], ACT.Exp).then_inc(expo, 1)

            @block.tensor
            def _(pe):
                pe.wait_ge(aux, 96)
                pe.wait_ge(chosen, 1)
                for n in range(NB):
                    for q in range(n):
                        nc.tensor.matmul(pR[:, n], core.ones[:], A[:, q], start=(q == 0), stop=False)
                    nc.tensor.matmul(pR[:, n], before[:], A[:, n], start=(n == 0), stop=True)
                for n in range(NB):
                    last = nc.tensor.matmul(pC[:, 0:EXPERTS], core.ones[:], A[:, n], start=(n == 0),
                                            stop=(n == NB - 1))
                last.then_inc(ranked, 1)
                pe.wait_ge(back, 16)
                nc.tensor.transpose(pL[:, 0:P], li[:], core.ident[:]).then_inc(turned, 1)

            @block.vector
            def _(dve):
                chain = Chain(dve, dch)

                def first_max(out, key, x, value, table, width):
                    chain(nc.vector.tensor_reduce(value, x, AX_X, ALU.max))
                    chain(nc.vector.tensor_tensor(key, x, value.unsqueeze(2).to_broadcast([P, NB, width]),
                                                  ALU.is_equal))
                    chain(nc.vector.tensor_tensor(key, key, table.unsqueeze(1).to_broadcast([P, NB, width]),
                                                  ALU.mult))
                    chain(nc.vector.tensor_reduce(m[:, 7], key, AX_X, ALU.max))
                    chain(nc.vector.tensor_tensor(out, key, m[:, 7].unsqueeze(2).to_broadcast([P, NB, width]),
                                                  ALU.is_equal))

                nc.vector.memset(zero[:], 0.0).then_inc(zeroed, 1)
                dve.wait_ge(aux, 96)
                chain(nc.vector.tensor_tensor(logits[:], logits[:], br[:].unsqueeze(1).to_broadcast([P, NB, 36]),
                                              ALU.add))
                gl = logits[:, :, 0:G]
                first_max(go[:], gk[:], gl, m[:, 0], desc[:, 32 - G:32], G)
                nc.vector.tensor_tensor(gx[:], gl, m[:, 0].unsqueeze(2).to_broadcast([P, NB, G]),
                                        ALU.subtract).then_inc(expo, 1)
                chain(nc.vector.tensor_scalar(gk[:], go[:], -1.0, 1.0e30, ALU.add, ALU.mult))
                e4 = em[:].rearrange("p n (g e) -> p n g e", g=G)
                chain(nc.vector.tensor_tensor(e4, logits[:, :, G:].rearrange("p n (g e) -> p n g e", g=G),
                                              go[:].unsqueeze(3).to_broadcast([P, NB, G, EPG]), ALU.mult))
                chain(nc.vector.tensor_tensor(e4, e4, gk[:].unsqueeze(3).to_broadcast([P, NB, G, EPG]), ALU.add))
                first_max(o1[:], ek[:], em[:], m[:, 1], desc[:], EXPERTS)
                chain(nc.vector.scalar_tensor_tensor(out=em[:], in0=o1[:], scalar=-3.0e30, in1=em[:], op0=ALU.mult,
                                                     op1=ALU.add))
                first_max(o2[:], ek[:], em[:], m[:, 2], desc[:], EXPERTS)
                nc.vector.tensor_tensor(A[:], o1[:], o2[:], ALU.add).then_inc(chosen, 1)
                dve.wait_ge(expo, 2)
                chain(nc.vector.tensor_reduce(m[:, 3], gx[:], AX_X, ALU.add))
                nc.vector.tensor_tensor(m[:, 5], m[:, 2], m[:, 1], ALU.subtract).then_inc(expo, 1)
                dve.wait_ge(expo, 4)
                chain(nc.vector.scalar_tensor_tensor(out=m[:, 4], in0=m[:, 5], scalar=1.0, in1=m[:, 3], op0=ALU.add,
                                                     op1=ALU.mult))
                chain(nc.vector.reciprocal(gate[:, :, 0], m[:, 4]))
                chain(nc.vector.tensor_tensor(gate[:, :, 1], gate[:, :, 0], m[:, 5], ALU.mult))
                dve.wait_ge(ranked, 1)
                chain(nc.vector.tensor_copy(rk[:], pR[:]))
                chain(nc.vector.tensor_scalar(rr[:], rk[:], float(P), None, ALU.is_ge))
                for r in (2, 3):
                    chain(nc.vector.scalar_tensor_tensor(out=rr[:], in0=rk[:], scalar=float(r * P), in1=rr[:],
                                                         op0=ALU.is_ge, op1=ALU.add))
                chain(nc.vector.scalar_tensor_tensor(out=rk[:], in0=rr[:], scalar=float((EXPERTS - 1) * P), in1=rk[:],
                                                     op0=ALU.mult, op1=ALU.add))
                chain(nc.vector.tensor_tensor(rk[:], rk[:], eoff[:].unsqueeze(1).to_broadcast([P, NB, EXPERTS]),
                                              ALU.add))
                for c, o in enumerate((o1, o2)):
                    chain(nc.vector.tensor_tensor(ek[:], o[:], rk[:], ALU.mult))
                    chain(nc.vector.tensor_reduce(posf[:, c * NB:(c + 1) * NB], ek[:], AX_X, ALU.add))
                nc.vector.tensor_copy(pos[:], posf[:]).then_inc(placed, 1)
                chain(nc.vector.tensor_reduce(m[:, 6, 0:1], pC[:, 0:EXPERTS], AX_X, ALU.max))
                chain(nc.vector.tensor_copy(most[:], m[:, 6, 0:1]))
                chain(nc.vector.memset(ix[:, P:P + 1], 0))
                dve.wait_ge(turned, 1)
                nc.vector.tensor_copy(ix[:, 0:P], pL[:, 0:P])


def experts_stage(core, most, ix):
    nc, dram = core.nc, core.dram
    with ExitStack() as ctx:
        def sb(n, shape, dt=F32):
            return ctx.enter_context(nc.sbuf_tensor("ex_" + n, shape, dt))
        ixc = sb("ix", [P, 2], I32)
        hg = sb("rows", [P, 2, D])
        hgT = sb("rowsT", [P, KT, P])
        sa, hid, hidT = sb("silu", [P, 2, FF]), sb("hidden", [P, 2, FF]), sb("hiddenT", [P, 2, FF])
        ys = sb("y", [P, 2, D])
        pG = ctx.enter_context(nc.psum_tensor("ex_p_gu", [P, 2, 512], F32))
        pT = ctx.enter_context(nc.psum_tensor("ex_p_T", [P, 2, 512], F32))
        pH = ctx.enter_context(nc.psum_tensor("ex_p_H", [P, 512], F32))
        pY = ctx.enter_context(nc.psum_tensor("ex_p_Y", [P, 2, 512], F32))
        hg_in = [core.sem("rows_in"), core.sem("rows_in")]
        y_out = [core.sem("y_stored"), core.sem("y_stored")]
        ix_ready, t_done, ta_out, tb_out, gu_done, silu_done, hid_done, th_done, hT_done, d_done, ya, yb = (
            core.sem(n) for n in ("ix_ready", "rows_turned", "turned_a", "turned_b", "gate_up", "silu", "hidden",
                                  "hidden_turned", "hiddenT", "down", "y_a", "y_b"))
        gw = [[core.sem(f"gate_up_in_{e}{h}") for h in range(2)] for e in range(2)]
        dw = [core.sem(f"down_in_{e}") for e in range(2)]
        dch, ach = core.sem("dve_chain"), core.sem("act_chain")

        def gu(e):
            return core.wide(4 * e, 4, 2 * FF)

        def dn(e):
            return core.wide(8 + 2 * e, 2, D)

        with nc.Block() as block:
            @block.sync
            def _(sp):
                def fetch(x):
                    gu_src = [dram["w_gu"][bass.ds(x, 1), :, 4 * h:4 * h + 4, :].rearrange("x p k c -> p (x k) c")
                              for h in range(2)]
                    return gu_src, dram["w_dn"][bass.ds(x, 1)].rearrange("x p k c -> p (x k) c")

                def load_gu(e, gu_src):
                    for h in range(2):
                        sp.dma_start(gu(e)[:, 4 * h:4 * h + 4, :], gu_src[h]).then_inc(gw[e][h], 16)

                def store(dst, e, value):
                    sp.wait_ge(ya, value)
                    sp.wait_ge(yb, value)
                    sp.dma_start(dst, ys[:, e]).then_inc(y_out[e], 16)

                def run(r):
                    first, n = r * EXPERTS, EXPERTS
                    if not isinstance(r, int):
                        sp.wait_ge(gu_done, first)
                        sp.wait_ge(d_done, first)
                    for e in range(2):
                        gu_src, dn_src = fetch(e)
                        load_gu(e, gu_src)
                        sp.dma_start(dn(e), dn_src).then_inc(dw[e], 16)
                    with sp.Fori(0, n // 2 - 1) as i:
                        for e in range(2):
                            u = i * 2 + (first + e)
                            gu_src, dn_src = fetch(i * 2 + (2 + e))
                            dst = core.Y[bass.ds(sp.snap(u * P), P), :]
                            done, stored = sp.snap(u + 1), sp.snap(u + 2)
                            sp.wait_ge(gu_done, done)
                            load_gu(e, gu_src)
                            sp.wait_ge(d_done, done)
                            sp.dma_start(dn(e), dn_src).then_inc(dw[e], 16)
                            store(dst, e, stored)
                    for e in range(2):
                        u = first + n - 2 + e
                        store(core.Y[bass.ds(u * P, P), :], e, u + 2)

                run(0)
                with sp.If(sp.value_load(most[0:1, 0:1], min_val=0, max_val=T) > P):
                    with sp.Fori(1, T // P) as r:
                        run(r)
                    for e in range(2):
                        sp.wait_ge(y_out[e], 16 * (2 * EXPERTS) + 16)
                for e in range(2):
                    sp.wait_ge(y_out[e], 16 * (EXPERTS // 2) + 16)

            @block.gpsimd
            def _(pool):
                def gather(u, e):
                    col_ = ix[:, u:u + 1] if isinstance(u, int) else ix[:, bass.ds(u, 1)]
                    pool.wait_ge(t_done, u + 1)
                    chain(nc.gpsimd.tensor_copy(ixc[:, e:e + 1], col_))
                    nc.gpsimd.indirect_dma_start(
                        out=hg[:, e, :], out_offset=None, in_=core.h_rows[:],
                        in_offset=bass.IndirectOffsetOnAxis(ap=ixc[:, e:e + 1], axis=0)).then_inc(hg_in[e], 16)

                def run(r):
                    first, n = r * EXPERTS, EXPERTS
                    with pool.Fori(0, n // 2) as i:
                        for e in range(2):
                            u = pool.snap(i * 2 + (first + e + 1))
                            gather(u, 1 - e)
                        chain.restart()
                chain = Chain(pool, ix_ready)
                gather(0, 0)
                chain.restart()
                run(0)
                with pool.If(pool.value_load(most[0:1, 0:1], min_val=0, max_val=T) > P):
                    with pool.Fori(1, T // P) as r:
                        run(r)

            @block.tensor
            def _(pe):
                def turn(u, e, seq):
                    pe.wait_ge(hg_in[e], seq)
                    pe.wait_ge(ta_out, u + 1)
                    pe.wait_ge(tb_out, u + 1)
                    for k in range(KT):
                        last = nc.tensor.transpose(pT[:, k // 4, (k % 4) * P:(k % 4 + 1) * P],
                                                   hg[:, e, k * P:(k + 1) * P], core.ident[:])
                    last.then_inc(t_done, 1)

                def gate_up(u, e, w):
                    pe.wait_ge(ta_out, u + 2)
                    pe.wait_ge(tb_out, u + 2)
                    pe.wait_ge(hid_done, u + 1)
                    for k in range(KT):
                        if k % 4 == 0:
                            pe.wait_ge(gw[e][k // 4], w)
                        last = nc.tensor.matmul(pG[:, e, :], hgT[:, k, :], gu(e)[:, k, :], start=(k == 0),
                                                stop=(k == KT - 1))
                    last.then_inc(gu_done, 1)

                def turn_hidden(u, e):
                    pe.wait_ge(hid_done, u + 3)
                    pe.wait_ge(hT_done, u + 1)
                    for f in range(FF // P):
                        last = nc.tensor.transpose(pH[:, f * P:(f + 1) * P], hid[:, e, f * P:(f + 1) * P],
                                                   core.ident[:])
                    last.then_inc(th_done, 1)

                def down(u, e, w):
                    pe.wait_ge(dw[e], w)
                    pe.wait_ge(hT_done, u + 2)
                    pe.wait_ge(ya, u + 1)
                    pe.wait_ge(yb, u + 1)
                    for half in range(2):
                        for f in range(FF // P):
                            last = nc.tensor.matmul(pY[:, half, :], hidT[:, e, f * P:(f + 1) * P],
                                                    dn(e)[:, f, half * 512:half * 512 + 512], start=(f == 0),
                                                    stop=(f == FF // P - 1))
                    last.then_inc(d_done, 1)

                def run(r):
                    first, n = r * EXPERTS, EXPERTS
                    h = r * (EXPERTS // 2)
                    gate_up(first, 0, 16 * (h + 1))
                    turn(first + 1, 1, 16 * (h + 1))
                    turn_hidden(first, 0)
                    with pe.Fori(0, n // 2 - 1) as i:
                        u = pe.snap(i * 2 + (first + 1))
                        w = pe.snap(i * 16 + 16 * (h + 1))
                        gate_up(u, 1, w)
                        turn(u + 1, 0, w + 16)
                        down(u - 1, 0, w)
                        turn_hidden(u, 1)
                        gate_up(u + 1, 0, w + 16)
                        turn(u + 2, 1, w + 16)
                        down(u, 1, w)
                        turn_hidden(u + 1, 0)
                    u, w = first + n - 1, 16 * (h + n // 2)
                    gate_up(u, 1, w)
                    turn(u + 1, 0, w + 16)
                    down(u - 1, 0, w)
                    turn_hidden(u, 1)
                    down(u, 1, w)

                turn(0, 0, 16)
                run(0)
                with pe.If(pe.value_load(most[0:1, 0:1], min_val=0, max_val=T) > P):
                    with pe.Fori(1, T // P) as r:
                        run(r)

            @block.scalar
            def _(act):
                def copy_rows(u):
                    act.wait_ge(t_done, u + 3)
                    act.wait_ge(gu_done, u)
                    nc.scalar.copy(hgT[:, 0:4, :].rearrange("p k c -> p (k c)"), pT[:, 0, :]).then_inc(ta_out, 1)

                def silu(u, e):
                    act.wait_ge(gu_done, u + 1)
                    act.wait_ge(hid_done, u + 1)
                    nc.scalar.activation(sa[:, e], pG[:, e, 0:FF], ACT.Silu).then_inc(silu_done, 1)

                def copy_y(u, e, w):
                    act.wait_ge(d_done, u + 1)
                    act.wait_ge(y_out[e], w)
                    nc.scalar.copy(ys[:, e, 0:512], pY[:, 0, :]).then_inc(ya, 1)

                def run(r):
                    first, n = r * EXPERTS, EXPERTS
                    h = r * (EXPERTS // 2)
                    silu(first, 0)
                    copy_rows(first + 1)
                    with act.Fori(0, n // 2 - 1) as i:
                        u = act.snap(i * 2 + (first + 1))
                        w = act.snap(i * 16 + 16 * (h + 1))
                        silu(u, 1)
                        copy_rows(u + 1)
                        copy_y(u - 1, 0, w)
                        silu(u + 1, 0)
                        copy_rows(u + 2)
                        copy_y(u, 1, w)
                    u, w = first + n - 1, 16 * (h + n // 2)
                    silu(u, 1)
                    copy_rows(u + 1)
                    copy_y(u - 1, 0, w)
                    copy_y(u, 1, w)

                act.wait_ge(t_done, 3)
                nc.scalar.copy(hgT[:, 0:4, :].rearrange("p k c -> p (k c)"), pT[:, 0, :]).then_inc(ta_out, 1)
                run(0)
                with act.If(act.value_load(most[0:1, 0:1], min_val=0, max_val=T) > P):
                    with act.Fori(1, T // P) as r:
                        run(r)

            @block.vector
            def _(dve):
                chain = Chain(dve, dch)

                def copy_rows(u):
                    dve.wait_ge(t_done, u + 3)
                    if not (isinstance(u, int) and u == 0):
                        dve.wait_ge(gu_done, u)
                    nc.vector.tensor_copy(hgT[:, 4:8, :].rearrange("p k c -> p (k c)"), pT[:, 1, :]).then_inc(tb_out, 1)

                def hidden(u, e):
                    dve.wait_ge(silu_done, u + 1)
                    if not (isinstance(u, int) and u == 0):
                        dve.wait_ge(th_done, u)
                    nc.vector.tensor_tensor(hid[:, e], sa[:, e], pG[:, e, FF:2 * FF], ALU.mult).then_inc(hid_done, 1)

                def copy_hidden(u, e):
                    dve.wait_ge(th_done, u + 1)
                    nc.vector.tensor_copy(hidT[:, e], pH[:, 0:FF]).then_inc(hT_done, 1)

                def copy_y(u, e, w):
                    dve.wait_ge(d_done, u + 1)
                    dve.wait_ge(y_out[e], w)
                    nc.vector.tensor_copy(ys[:, e, 512:1024], pY[:, 1, :]).then_inc(yb, 1)

                def run(r):
                    first, n = r * EXPERTS, EXPERTS
                    h = r * (EXPERTS // 2)
                    hidden(first, 0)
                    copy_rows(first + 1)
                    copy_hidden(first, 0)
                    with dve.Fori(0, n // 2 - 1) as i:
                        u = dve.snap(i * 2 + (first + 1))
                        w = dve.snap(i * 16 + 16 * (h + 1))
                        hidden(u, 1)
                        copy_rows(u + 1)
                        copy_y(u - 1, 0, w)
                        copy_hidden(u, 1)
                        hidden(u + 1, 0)
                        copy_rows(u + 2)
                        copy_y(u, 1, w)
                        copy_hidden(u + 1, 0)
                    u, w = first + n - 1, 16 * (h + n // 2)
                    hidden(u, 1)
                    copy_rows(u + 1)
                    copy_y(u - 1, 0, w)
                    copy_hidden(u, 1)
                    copy_y(u, 1, w)

                for s, n in ((t_done, 2), (ta_out, 1), (tb_out, 1), (hid_done, 2), (hT_done, 1), (ya, 1), (yb, 1), (y_out[0], 16),
                             (y_out[1], 16)):
                    chain(nc.vector.tensor_copy(core.spare[:, 1:2], core.spare[:, 0:1]))
                    dve.engine_nop().then_inc(s, n)
                copy_rows(0)
                run(0)
                with dve.If(dve.value_load(most[0:1, 0:1], min_val=0, max_val=T) > P):
                    with dve.Fori(1, T // P) as r:
                        run(r)


def combine_stage(core, x_rows, gate, pos, most, out):
    nc = core.nc
    with (nc.sbuf_tensor("cb_g", [P, NB, 2, D], F32) as g, nc.Block() as block):
        got = [core.sem(f"row_{n}") for n in range(NB)]
        summed, stored, dch = core.sem("summed"), core.sem("stored"), core.sem("dve_chain")

        @block.gpsimd
        def _(pool):
            def gather(rows):
                for n in range(NB):
                    for c in range(2):
                        nc.gpsimd.indirect_dma_start(
                            out=g[:, n, c, :], out_offset=None, in_=rows,
                            in_offset=bass.IndirectOffsetOnAxis(ap=pos[:, c * NB + n:c * NB + n + 1], axis=0))\
                            .then_inc(got[n], 16)

            more = pool.value_load(most[0:1, 0:1], min_val=0, max_val=T)
            with pool.If(more > P):
                gather(core.Y[:])
            with pool.Else():
                gather(core.Y[0:EXPERTS * P])

        @block.vector
        def _(dve):
            chain = Chain(dve, dch)
            for n in range(NB):
                dve.wait_ge(got[n], 32)
                chain(nc.vector.scalar_tensor_tensor(out=x_rows[:, n], in0=g[:, n, 0], scalar=gate[:, n, 0:1],
                                                     in1=x_rows[:, n], op0=ALU.mult, op1=ALU.add))
                nc.vector.scalar_tensor_tensor(out=x_rows[:, n], in0=g[:, n, 1], scalar=gate[:, n, 1:2],
                                               in1=x_rows[:, n], op0=ALU.mult, op1=ALU.add).then_inc(summed, 1)

        @block.sync
        def _(sp):
            for n in range(NB):
                sp.wait_ge(summed, n + 1)
                sp.dma_start(out[n * P:(n + 1) * P, :], x_rows[:, n]).then_inc(stored, 16)
            sp.wait_ge(stored, 16 * NB)


def load(core, pairs):
    arrived = core.sem("loaded")
    with core.nc.Block() as block:
        @block.sync
        def _(sp):
            for dst, src in pairs:
                sp.dma_start(dst, src).then_inc(arrived, 16)
            sp.wait_ge(arrived, 16 * len(pairs))


def store_rows(core, rows):
    stored = core.sem("stored")
    with core.nc.Block() as block:
        @block.sync
        def _(sp):
            sp.dma_start(core.h_rows.rearrange("(n p) d -> p n d", p=P), rows[:]).then_inc(stored, 16)
            sp.wait_ge(stored, 16)


def build(nc, dram, out):
    with ExitStack() as ctx:
        core = Core(nc, ctx, dram)
        load_constants(core, ctx)
        with ExitStack() as first:
            yaT = first.enter_context(nc.sbuf_tensor("yaT", [P, KT, T], F32))
            rms_norm(core, core.xT, core.hT, KT, T, "norm_w")
            gla_stage(core, yaT)
            core.recycle()
            ybT = first.enter_context(nc.sbuf_tensor("ybT", [P, KT, T], F32))
            spatial_stage(core, ybT)
            mT = first.enter_context(nc.sbuf_tensor("mT", [P, KT, T], F32))
            merge_stage(core, yaT, ybT, mT)
            residual_stage(core, "w_out", KT, mT)
        core.recycle()
        rms_norm(core, core.xT, core.xT, KT, T, "final")

        with ExitStack() as mix:
            def sb(name, shape):
                return mix.enter_context(nc.sbuf_tensor(name, shape, F32))
            rms_norm(core, core.xT, core.hT, KT, T, "mix")
            y2T = sb("y2T", [P, KT, T])
            qkT = sb("qkT", [P, 8, T])
            bias = sb("bias", [P, NB, T])
            v2 = sb("v2", [P, NB, T])
            y2 = sb("y2", [P, NB, T])
            with ExitStack() as rope:
                core.cos, core.sin, core.rot, core.pair_ones = (
                    rope.enter_context(nc.sbuf_tensor(n, s, F32)) for n, s in (
                        ("cos", [P, T]), ("sin", [P, T]), ("rot", [P, P]), ("pair_ones", [P, P])))
                load(core, [(core.cos[:], dram["cos"][:]), (core.sin[:], dram["sin"][:]), (core.rot[:], dram["rot"][:]),
                            (core.pair_ones[:], dram["pair_ones"][:])])
                with (nc.sbuf_tensor("kiT", [P, 1, T], F32) as kiT, nc.sbuf_tensor("qiT", [P, 4, T], F32) as qiT,
                      nc.sbuf_tensor("wi", [P, NB, 8], F32) as wi):
                    rope_stage(core, "w_ki", 1, "idx_norm", kiT, 0, 1)
                    rope_stage(core, "w_qi", 4, None, qiT, 0, 2)
                    natural_stage(core, "w_wi", core.hT, KT, NB, 8, wi)
                    index_stage(core, qiT, kiT, wi, bias)
                core.recycle()
                rope_stage(core, "w_q", 4, "q_norm", qkT, 0, 2)
                rope_stage(core, "w_k", 4, "k_norm", qkT, 4, 2)
            pool_stage(core, y2T)
            natural_stage(core, "w_v2", core.hT, KT, NB, T, v2)
            attention_stage(core, "attn_", qkT, qkT[:, 4:8], v2, y2, 4, 64, 64 ** -0.5,
                            [P * (b + 1) for b in range(NB)], bias)
            core.recycle()
            turn_stage(core, y2, NB, 4, y2T, 4)
            residual_stage(core, "w_out2", KT, y2T)

        with ExitStack() as cross:
            def sb(name, shape):
                return cross.enter_context(nc.sbuf_tensor(name, shape, F32))
            rms_norm(core, core.xT, core.hT, KT, T, "xattn")
            memT = sb("memT", [P, KT, MEM])
            load(core, [(memT[:], dram["memT"][:])])
            rms_norm(core, memT, memT, KT, MEM, "mem")
            qmT, kmT = sb("qmT", [P, 4, T]), sb("kmT", [P, 4, MEM])
            vm, ym, omT = sb("vm", [P, MEM // P, T]), sb("ym", [P, NB, T]), sb("omT", [P, 4, T])
            project_stage(core, "w_xq", core.hT, KT, 4, T, qmT)
            norm_heads_stage(core, qmT, 4, T, "xq_norm")
            project_stage(core, "w_xk", memT, KT, 4, MEM, kmT)
            core.recycle()
            norm_heads_stage(core, kmT, 4, MEM, "xk_norm")
            natural_stage(core, "w_xv", memT, KT, MEM // P, T, vm)
            attention_stage(core, "cross_", qmT, kmT, vm, ym, 4, P, float(P) ** -0.5, [MEM] * NB, None)
            turn_stage(core, ym, NB, 4, omT, 0)
            residual_stage(core, "w_xo", 4, omT)
        core.recycle()

        with ExitStack() as moe:
            def sb(name, shape, dt=F32):
                return moe.enter_context(nc.sbuf_tensor(name, shape, dt))
            core.h_rows = nc.dram_tensor("h_rows", [T, D], F32).ap()
            core.list = nc.dram_tensor("token_list", [P * (P + 1), 1], F32).ap()
            core.Y = nc.dram_tensor("expert_rows", [P * P, D], F32).ap()
            x_rows = sb("x_rows", [P, NB, D])
            logits, gate = sb("logits", [P, NB, 36]), sb("gate", [P, NB, 2])
            pos, most, ix = sb("pos", [P, 2 * NB], I32), sb("most", [P, 1], I32), sb("ix_all", [P, P + 1], I32)
            rms_norm(core, core.xT, core.hT, KT, T, "ffn")
            rows_stage(core, core.hT, x_rows)
            store_rows(core, x_rows)
            rows_stage(core, core.xT, x_rows)
            natural_stage(core, "w_router", core.hT, KT, NB, 36, logits)
            route_stage(core, logits, gate, pos, most, ix)
            core.recycle()
            experts_stage(core, most, ix)
            core.recycle()
            combine_stage(core, x_rows, gate, pos, most, out)



def _vec(a):
    return np.asarray(a).reshape(-1, P).T


def _tiles(w):
    k, c = w.shape
    return np.ascontiguousarray(w.reshape(k // P, P, c // P, P).transpose(2, 1, 0, 3)).reshape(c // P, P, k)


def _rows(w):
    return np.ascontiguousarray(w.reshape(w.shape[0] // P, P, w.shape[1]).transpose(1, 0, 2))


def layout(inputs):
    a = {k: np.asarray(v) for k, v in inputs.items()}
    arr = {"xT": _rows(np.ascontiguousarray(a["x"][0].T))}
    w = _tiles(a["w_in"][0])
    order = [[8 + h, 16 + h, h, 32 + h, 24 + h] for h in range(HEADS)]
    arr["w_gla"] = np.ascontiguousarray(w[np.array(order)].transpose(0, 2, 1, 3))
    arr["w_ug"] = np.ascontiguousarray(
        w[np.array([[40 + g, 56 + g, 41 + g, 57 + g] for g in range(0, HEADS, 2)])].transpose(0, 2, 1, 3))
    arr["w_v"] = _rows(a["w_in"][0][:, 6 * D:7 * D]).reshape(P, -1)
    arr["w_s"] = np.ascontiguousarray(a["w_s"][0].transpose(0, 2, 1))
    arr["b_s"] = a["b_s"][0].reshape(1, -1)
    arr["ln_w"], arr["ln_b"] = a["ln_w"], a["ln_b"]
    wa, wb = _tiles(a["w_proj_a"][0]), _tiles(a["w_proj_b"][0])
    arr["w_merge"] = np.ascontiguousarray(np.stack([w[64:72], wa, w[72:80], wb], 1).transpose(0, 2, 1, 3))
    arr["w_out"] = _tiles(a["w_out"][0])
    w2 = a["w_in_2"][0]
    t2 = _tiles(w2[:, 0:2560])
    arr["w_pool_in"], arr["w_q"], arr["w_k"], arr["w_qi"] = t2[0:4], t2[4:8], t2[8:12], t2[16:20]
    arr["w_ki"] = _tiles(np.tile(w2[:, 2560:2624], (1, 2)))
    arr["w_wi"] = _rows(w2[:, 2624:2632]).reshape(P, -1)
    arr["w_v2"] = _rows(w2[:, 1536:2048]).reshape(P, -1)
    arr["pool_w"] = np.ascontiguousarray(a["pool_w_2"][0].transpose(1, 0, 2))
    arr["w_out2"] = _tiles(a["w_out_2"][0])
    arr["memT"] = _rows(np.ascontiguousarray(a["mem_2"][0].T))
    arr["w_xq"] = _tiles(a["xattn_wq_2"][0])
    arr["w_xk"] = _tiles(a["xattn_wkv_2"][0][:, 0:512])
    arr["w_xv"] = _rows(a["xattn_wkv_2"][0][:, 512:1024]).reshape(P, -1)
    arr["w_router"] = _rows(np.concatenate([a["router_group_w_2"][0], a["router_expert_w_2"][0]], 1)).reshape(P, -1)
    arr["router_b"] = np.concatenate([a["router_group_b_2"], a["router_expert_b_2"]], 1)
    gw, uw, dw = (a[f"expert_w_{n}_2"][0] for n in ("gate", "up", "down"))
    gu = np.concatenate([gw.reshape(EXPERTS, KT, P, FF), uw.reshape(EXPERTS, KT, P, FF)], 3)
    arr["w_gu"] = np.ascontiguousarray(gu.transpose(0, 2, 1, 3))
    arr["w_dn"] = np.ascontiguousarray(dw.reshape(EXPERTS, FF // P, P, D).transpose(0, 2, 1, 3))
    arr["w_xo"] = _tiles(a["xattn_wo_2"][0])
    parts = {
        "norm_w": _vec(a["norm_w"]), "lb": np.concatenate([_vec(a["lower_bounds"][0, 0]), _vec(a["lower_bounds"][0, 1])], 1),
        "gnorm": _vec(a["gnorm_w"]), "final": _vec(a["final_norm_w"]), "mix": _vec(a["mix_norm_2"]),
        "pool_scale": _vec(a["pool_scale_2"]), "q_norm": np.tile(a["q_norm_2"].reshape(-1, 1), (2, 1)),
        "k_norm": np.tile(a["k_norm_2"].reshape(-1, 1), (2, 1)),
        "idx_norm": np.tile(a["idx_k_norm_2"].reshape(-1, 1), (2, 1)), "xattn": _vec(a["xattn_norm_2"]),
        "mem": _vec(a["mem_norm_2"]), "xq_norm": _vec(a["xattn_q_norm_2"]), "xk_norm": _vec(a["xattn_k_norm_2"]),
        "ffn": _vec(a["ffn_norm_2"]),
    }
    arr["cols"] = np.ascontiguousarray(np.concatenate([parts[n] for n in COLS_N], 1))
    return arr


def shape_constants():
    s = np.arange(P)
    keep = np.ones((P, T), np.float32)
    keep[:, ::P] = 0.0
    masks = np.zeros((P, LEVELS + 1, P), np.int32)
    for l in range(LEVELS):
        half = P >> (l + 1)
        masks[:, l] = ((s[:, None] // (2 * half)) == (s[None] // (2 * half))) & ((s[:, None] // half) != (s[None] // half))
    masks[:, LEVELS] = np.eye(P)
    half = 32
    inv = (10000.0 ** (-np.arange(0, 2 * half, 2, dtype=np.float32) / np.float32(2 * half))).astype(np.float32)
    ang = np.arange(T, dtype=np.float32)[:, None] * np.tile(inv, 4)[None, :]
    rot = np.zeros((P, P), np.float32)
    for m in range(P):
        if m % 64 < half:
            rot[m + half, m] = -1.0
        else:
            rot[m - half, m] = 1.0
    extra = {
        "cos": np.ascontiguousarray(np.cos(ang).T.astype(np.float32)),
        "sin": np.ascontiguousarray(np.sin(ang).T.astype(np.float32)),
        "rot": rot, "pair_ones": np.kron(np.eye(2), np.ones((64, 64))).astype(np.float32),
        "hide": np.where((s[:, None] // 64) < (s[None] // 64), HIDDEN, 0.0).astype(np.float32),
        "pool_inv": np.ascontiguousarray(np.broadcast_to(np.stack(
            [1.0 / np.minimum(np.arange(1, 17), 2 ** (g + 1)) for g in range(4)]).astype(np.float32), (P, 4, 16))),
    }
    table = np.zeros((P, 64 + NB), np.float32)
    table[:, 0:32] = np.arange(32, 0, -1)
    table[:, 32:64] = np.arange(32) * P
    table[:, 64:] = np.arange(NB)[None] * P + s[:, None]
    extra["moe_table"] = table
    extra["before"] = (s[:, None] < s[None]).astype(np.float32)
    return {**extra, "ident": np.eye(P, dtype=np.float32), "scan_keep": keep, "level_masks": masks}


def kernel(**inputs):
    import concourse.bacc as _bacc
    from concourse.bass_utils import run_bass_kernel_spmd as _run

    nc = _bacc.Bacc("TRN2", target_bir_lowering=False, num_devices=1)
    arrays = {f"in_{k}": v for k, v in {**layout(inputs), **shape_constants()}.items()}
    dram = {k[3:]: nc.dram_tensor(k, v.shape, mybir.dt.from_np(v.dtype), kind="ExternalInput").ap()
            for k, v in arrays.items()}
    out = nc.dram_tensor("out", [T, D], F32, kind="ExternalOutput").ap()
    build(nc, dram, out)
    r = _run(nc, [arrays], core_ids=[0])
    return r.results[0]["out"].reshape(1, T, D)
```
